# Optimizing a Trainium2 kernel written in Bass

```python
import math
import jax, jax.numpy as jnp
from jax import lax
import numpy as np

D_MODEL = 1024
BATCH = 1
SEQ = 256
DEPTH = 2

P_DIM = 256
D_FF = 2816
ML_HEADS = 4
ML_QK_DIM = 64
ML_V_DIM = 128
ML_CHUNK = 64
SW_Q_HEADS = 8
SW_KV_HEADS = 2
SW_HEAD_DIM = 64
WINDOW = 128
REL_BUCKETS = 32
REL_MAX_DIST = 128
EPS = 1e-6

ML_QK_W = ML_HEADS * ML_QK_DIM
ML_V_W = ML_HEADS * ML_V_DIM
SW_Q_W = SW_Q_HEADS * SW_HEAD_DIM
SW_KV_W = SW_KV_HEADS * SW_HEAD_DIM
SPLITS = (ML_QK_W, ML_QK_W, ML_V_W, ML_V_W, ML_HEADS, ML_HEADS, SW_Q_W, SW_KV_W, SW_KV_W, D_MODEL, D_MODEL)
D_IN = 2 * ML_QK_W + 2 * ML_V_W + 2 * ML_HEADS + SW_Q_W + 2 * SW_KV_W + 2 * D_MODEL


def rmsnorm(x, g):
    xf = x.astype(jnp.float32)
    y = xf * lax.rsqrt(jnp.mean(xf * xf, axis=-1, keepdims=True) + EPS)
    return (y * g.astype(jnp.float32)).astype(x.dtype)

def swiglu_ffn(x, wi, wo):
    g, u = jnp.split(x @ wi, 2, axis=-1)
    return (jax.nn.silu(g) * u) @ wo

def t5_bucket(dist):
    max_exact = REL_BUCKETS // 2
    d = np.maximum(dist, 0)
    large = max_exact + (np.log(np.maximum(d, 1) / max_exact) / np.log(REL_MAX_DIST / max_exact)
                         * (REL_BUCKETS - max_exact)).astype(np.int32)
    large = np.minimum(large, REL_BUCKETS - 1)
    return np.where(d < max_exact, d, large).astype(np.int32)

def mlstm_chunkwise(q, k, v, i_pre, f_pre):
    B, S, H, dk = q.shape
    dv = v.shape[-1]
    L = ML_CHUNK
    NC = S // L
    f32 = jnp.float32
    qc = q.astype(f32).reshape(B, NC, L, H, dk)
    kc = (k.astype(f32) / math.sqrt(dk)).reshape(B, NC, L, H, dk)
    vc = v.astype(f32).reshape(B, NC, L, H, dv)
    log_i = jnp.swapaxes(i_pre.astype(f32).reshape(B, NC, L, H), 2, 3)
    log_f = jnp.swapaxes(jax.nn.log_sigmoid(f_pre.astype(f32)).reshape(B, NC, L, H), 2, 3)
    b = jnp.cumsum(log_f, axis=-1)
    g = b[..., -1]
    a = g[..., None] - b + log_i
    m_loc = jnp.max(a, axis=-1)
    w = jnp.exp(a - m_loc[..., None])
    C_loc = jnp.einsum('bnhl,bnlhk,bnlhv->bnhkv', w, kc, vc)
    n_loc = jnp.einsum('bnhl,bnlhk->bnhk', w, kc)

    def step(carry, xs):
        C, n, m = carry
        g_c, m_c, C_c, n_c = xs
        m_new = jnp.maximum(g_c + m, m_c)
        s_old = jnp.exp(g_c + m - m_new)
        s_new = jnp.exp(m_c - m_new)
        C_new = s_old[..., None, None] * C + s_new[..., None, None] * C_c
        n_new = s_old[..., None] * n + s_new[..., None] * n_c
        return (C_new, n_new, m_new), (C, n, m)

    init = (jnp.zeros((B, H, dk, dv), f32), jnp.zeros((B, H, dk), f32), jnp.zeros((B, H), f32))
    xs = (jnp.moveaxis(g, 1, 0), jnp.moveaxis(m_loc, 1, 0), jnp.moveaxis(C_loc, 1, 0), jnp.moveaxis(n_loc, 1, 0))
    _, (C_prev, n_prev, m_prev) = lax.scan(step, init, xs)
    C_prev = jnp.moveaxis(C_prev, 0, 1)
    n_prev = jnp.moveaxis(n_prev, 0, 1)
    m_prev = jnp.moveaxis(m_prev, 0, 1)

    causal = jnp.tril(jnp.ones((L, L), dtype=bool))
    D = b[..., :, None] - b[..., None, :] + log_i[..., None, :]
    D = jnp.where(causal, D, -jnp.inf)
    e = b + m_prev[..., None]
    m_t = jnp.maximum(jnp.max(D, axis=-1), e)
    W = jnp.exp(D - m_t[..., None]) * jnp.einsum('bnthd,bnshd->bnhts', qc, kc)
    s_inter = jnp.exp(e - m_t)
    num = (jnp.einsum('bnhts,bnshv->bnthv', W, vc)
           + jnp.swapaxes(s_inter, 2, 3)[..., None] * jnp.einsum('bnthd,bnhdv->bnthv', qc, C_prev))
    den = jnp.sum(W, axis=-1) + s_inter * jnp.einsum('bnthd,bnhd->bnht', qc, n_prev)
    denom = jnp.maximum(jnp.abs(den), jnp.exp(-m_t))
    h = num / jnp.swapaxes(denom, 2, 3)[..., None]
    return h.reshape(B, S, H, dv).astype(q.dtype)

def swa_sink_attention(q, k, v, q_gain, k_gain, sinks, rel_bias):
    B, S, Hq, d = q.shape
    Hkv = k.shape[2]
    G = Hq // Hkv
    Wn = WINDOW
    NB = S // Wn
    f32 = jnp.float32
    q = rmsnorm(q, q_gain)
    k = rmsnorm(k, k_gain)
    qb = q.astype(f32).reshape(B, NB, Wn, Hkv, G, d) * (d ** -0.5)
    kb = k.astype(f32).reshape(B, NB, Wn, Hkv, d)
    vb = v.astype(f32).reshape(B, NB, Wn, Hkv, d)
    shift = lambda t: jnp.concatenate([jnp.zeros_like(t[:, :1]), t[:, :-1]], axis=1)
    kk = jnp.concatenate([shift(kb), kb], axis=2)
    vv = jnp.concatenate([shift(vb), vb], axis=2)
    logits = jnp.einsum('bnqkgd,bnskd->bnkgqs', qb, kk)
    dist = np.arange(Wn)[:, None] + Wn - np.arange(2 * Wn)[None, :]
    in_window = (dist >= 0) & (dist < Wn)
    bias = rel_bias.astype(f32)[t5_bucket(dist)]
    bias = jnp.transpose(bias, (2, 0, 1)).reshape(Hkv, G, Wn, 2 * Wn)
    key_pos = np.arange(NB)[:, None] * Wn - Wn + np.arange(2 * Wn)[None, :]
    valid = in_window[None] & (key_pos >= 0)[:, None, :]
    logits = jnp.where(valid[None, :, None, None], logits + bias, -jnp.inf)
    sink = sinks.astype(f32).reshape(Hkv, G)[None, None, :, :, None, None]
    m = jnp.maximum(jnp.max(logits, axis=-1, keepdims=True), sink)
    pr = jnp.exp(logits - m)
    denom = jnp.sum(pr, axis=-1, keepdims=True) + jnp.exp(sink - m)
    out = jnp.einsum('bnkgqs,bnskd->bnqkgd', pr / denom, vv)
    return out.reshape(B, S, Hq * d).astype(q.dtype)

def first_inputs(seed: int = 0) -> dict:
    key = jax.random.key(seed)
    ks = jax.random.split(key, 24)
    f32 = jnp.float32
    nrm = lambda k, shape, fan_in: jax.random.normal(k, shape, f32) * (fan_in ** -0.5)
    gain = lambda k, shape: 1.0 + 0.05 * jax.random.normal(k, shape, f32)
    return {
        "x": jax.random.normal(ks[0], (BATCH, SEQ, D_MODEL), f32),
        "p": jax.random.normal(ks[1], (DEPTH, BATCH, SEQ, P_DIM), f32),
        "ffn1_norm": gain(ks[2], (DEPTH, D_MODEL)),
        "ffn1_wi": nrm(ks[3], (DEPTH, D_MODEL, 2 * D_FF), D_MODEL),
        "ffn1_wo": nrm(ks[4], (DEPTH, D_FF, D_MODEL), D_FF),
        "mix_norm": gain(ks[5], (DEPTH, D_MODEL)),
        "w_in": nrm(ks[6], (DEPTH, D_MODEL, D_IN), D_MODEL),
        "b_igate": 0.1 * jax.random.normal(ks[7], (DEPTH, ML_HEADS), f32),
        "b_fgate": jnp.linspace(3.0, 6.0, ML_HEADS, dtype=f32)[None, :] + 0.1 * jax.random.normal(ks[8], (DEPTH, ML_HEADS), f32),
        "ml_out_norm": gain(ks[9], (DEPTH, ML_HEADS, ML_V_DIM)),
        "q_norm": gain(ks[10], (DEPTH, SW_HEAD_DIM)),
        "k_norm": gain(ks[11], (DEPTH, SW_HEAD_DIM)),
        "sinks": 0.5 * jax.random.normal(ks[12], (DEPTH, SW_Q_HEADS), f32),
        "rel_bias": 0.5 * jax.random.normal(ks[13], (REL_BUCKETS, SW_Q_HEADS), f32),
        "w_a": nrm(ks[14], (DEPTH, ML_V_W, D_MODEL), ML_V_W),
        "w_b": nrm(ks[15], (DEPTH, SW_Q_W, D_MODEL), SW_Q_W),
        "w_out": nrm(ks[16], (DEPTH, D_MODEL, D_MODEL), D_MODEL),
        "ffn2_norm": gain(ks[17], (DEPTH, D_MODEL)),
        "ffn2_wi": nrm(ks[18], (DEPTH, D_MODEL, 2 * D_FF), D_MODEL),
        "ffn2_wo": nrm(ks[19], (DEPTH, D_FF, D_MODEL), D_FF),
        "ple_norm": gain(ks[20], (DEPTH, D_MODEL)),
        "w_ple_gate": nrm(ks[21], (DEPTH, D_MODEL, D_MODEL), D_MODEL),
        "w_ple": nrm(ks[22], (DEPTH, P_DIM, D_MODEL), P_DIM),
    }

def first_block(x, p, ffn1_norm, ffn1_wi, ffn1_wo, mix_norm, w_in, b_igate, b_fgate, ml_out_norm,
              q_norm, k_norm, sinks, rel_bias, w_a, w_b, w_out, ffn2_norm, ffn2_wi, ffn2_wo,
              ple_norm, w_ple_gate, w_ple):
    B, S, _ = x.shape
    offsets = [int(o) for o in np.cumsum(SPLITS)[:-1]]
    for i in range(DEPTH):
        x = x + 0.5 * swiglu_ffn(rmsnorm(x, ffn1_norm[i]), ffn1_wi[i], ffn1_wo[i])
        u = rmsnorm(x, mix_norm[i])
        z = u @ w_in[i]
        mq, mk, mv, mo, mi, mf, sq, sk, sv, ga, gb = jnp.split(z, offsets, axis=-1)
        hA = mlstm_chunkwise(mq.reshape(B, S, ML_HEADS, ML_QK_DIM),
                             mk.reshape(B, S, ML_HEADS, ML_QK_DIM),
                             mv.reshape(B, S, ML_HEADS, ML_V_DIM),
                             mi + b_igate[i], mf + b_fgate[i])
        hA = rmsnorm(hA, ml_out_norm[i]).reshape(B, S, ML_V_W)
        yA = (jax.nn.sigmoid(mo) * hA) @ w_a[i]
        hB = swa_sink_attention(sq.reshape(B, S, SW_Q_HEADS, SW_HEAD_DIM),
                                sk.reshape(B, S, SW_KV_HEADS, SW_HEAD_DIM),
                                sv.reshape(B, S, SW_KV_HEADS, SW_HEAD_DIM),
                                q_norm[i], k_norm[i], sinks[i], rel_bias)
        yB = hB @ w_b[i]
        mixed = jax.nn.sigmoid(ga) * yA + jax.nn.sigmoid(gb) * yB
        x = x + mixed @ w_out[i]
        x = x + 0.5 * swiglu_ffn(rmsnorm(x, ffn2_norm[i]), ffn2_wi[i], ffn2_wo[i])
        gate = jax.nn.sigmoid(rmsnorm(x, ple_norm[i]) @ w_ple_gate[i])
        x = x + gate * (p[i] @ w_ple[i])
    return x


D_MIX = D_MODEL
D_CONV = D_MIX // 4
D_POOL = D_MIX // 4
D_ATTN = D_MIX // 2
N_HEADS = 4
HEAD_DIM = D_ATTN // (2 * N_HEADS)
V_DIM = 2 * HEAD_DIM
CONV_WIDTH = 31
POOL_WINDOWS = (2, 4, 8, 16)
N_POOL_GROUPS = len(POOL_WINDOWS)
POOL_GROUP_DIM = D_POOL // N_POOL_GROUPS
D_FF_2 = 256 * ((8 * D_MODEL // 3 + 255) // 256)
D_IN_2 = 2 * D_CONV + D_POOL + 3 * D_ATTN
Q_BLOCK = 128
NORM_EPS = 1e-6


def rms_norm(x, g):
    xf = x.astype(jnp.float32)
    y = xf * lax.rsqrt(jnp.mean(xf * xf, axis=-1, keepdims=True) + NORM_EPS)
    return (y * g.astype(jnp.float32)).astype(x.dtype)

def layer_norm(x, g, b):
    xf = x.astype(jnp.float32)
    mu = jnp.mean(xf, axis=-1, keepdims=True)
    xc = xf - mu
    y = xc * lax.rsqrt(jnp.mean(xc * xc, axis=-1, keepdims=True) + NORM_EPS)
    return (y * g.astype(jnp.float32) + b.astype(jnp.float32)).astype(x.dtype)

def swiglu_ffn_2(h, w_gate, w_up, w_down):
    return (jax.nn.silu(h @ w_gate) * (h @ w_up)) @ w_down

def conformer_conv(u, w_dw, b_dw, ln_g, ln_b):
    a, gate = jnp.split(u, 2, axis=-1)
    z = a * jax.nn.sigmoid(gate)
    z = lax.conv_general_dilated(
        z, w_dw[:, None, :], window_strides=(1,),
        padding=((CONV_WIDTH // 2, CONV_WIDTH // 2),),
        dimension_numbers=("NWC", "WIO", "NWC"),
        feature_group_count=D_CONV) + b_dw
    return jax.nn.silu(layer_norm(z, ln_g, ln_b))

def multiscale_pool(u, w_grp, scale):
    B_, S_, _ = u.shape
    uf = u.astype(jnp.float32)
    cs = jnp.concatenate([jnp.zeros((B_, 1, D_POOL), jnp.float32), jnp.cumsum(uf, axis=1)], axis=1)
    t = jnp.arange(S_, dtype=jnp.int32)
    outs = []
    for g, w in enumerate(POOL_WINDOWS):
        sl = slice(g * POOL_GROUP_DIM, (g + 1) * POOL_GROUP_DIM)
        lo = jnp.clip(t - w // 2, 0, S_)
        hi = jnp.clip(t + w // 2, 0, S_)
        csg = cs[..., sl]
        win_sum = jnp.take(csg, hi, axis=1) - jnp.take(csg, lo, axis=1)
        cnt = (hi - lo).astype(jnp.float32)[None, :, None]
        outs.append(win_sum / cnt - uf[..., sl])
    d = jnp.stack(outs, axis=2)
    y = jnp.einsum("bsgc,gcd->bsgd", d, w_grp.astype(jnp.float32)).reshape(B_, S_, D_POOL)
    return (y * scale.astype(jnp.float32)).astype(u.dtype)

def diff_attention(q, k, v, lam, slopes):
    B_, S_ = q.shape[0], q.shape[1]
    n_blk = S_ // Q_BLOCK
    q_blocks = jnp.moveaxis(q.reshape(B_, n_blk, Q_BLOCK, N_HEADS, 2, HEAD_DIM), 1, 0)
    k_pos = jnp.arange(S_, dtype=jnp.int32)

    def block(args):
        q_blk, blk = args
        q_pos = blk * Q_BLOCK + jnp.arange(Q_BLOCK, dtype=jnp.int32)
        dist = jnp.abs(q_pos[:, None] - k_pos[None, :]).astype(jnp.float32)
        s = jnp.einsum("bqhcd,bkhcd->bhcqk", q_blk, k, preferred_element_type=jnp.float32)
        s = s - slopes[None, :, None, None, None] * dist
        p = jax.nn.softmax(s, axis=-1)
        a = p[:, :, 0] - lam * p[:, :, 1]
        return jnp.einsum("bhqk,bkhe->bqhe", a.astype(v.dtype), v)

    o = lax.map(block, (q_blocks, jnp.arange(n_blk, dtype=jnp.int32)))
    return jnp.moveaxis(o, 0, 1).reshape(B_, S_, N_HEADS, V_DIM)

def second_inputs(seed: int = 0) -> dict:
    key = jax.random.key(seed)
    ks = iter(jax.random.split(key, 32))

    def nrm(shape, scale):
        return jax.random.normal(next(ks), shape, jnp.float32) * scale

    def gain(shape):
        return 1.0 + 0.02 * jax.random.normal(next(ks), shape, jnp.float32)

    L = DEPTH
    return {
        "x": nrm((BATCH, SEQ, D_MODEL), 1.0),
        "ffn1_norm": gain((L, D_MODEL)),
        "ffn1_w_gate": nrm((L, D_MODEL, D_FF_2), D_MODEL ** -0.5),
        "ffn1_w_up": nrm((L, D_MODEL, D_FF_2), D_MODEL ** -0.5),
        "ffn1_w_down": nrm((L, D_FF_2, D_MODEL), D_FF_2 ** -0.5),
        "mix_norm": gain((L, D_MODEL)),
        "w_in": nrm((L, D_MODEL, D_IN_2), D_MODEL ** -0.5),
        "conv_dw": nrm((L, CONV_WIDTH, D_CONV), CONV_WIDTH ** -0.5),
        "conv_dw_bias": nrm((L, D_CONV), 0.02),
        "conv_ln_gain": gain((L, D_CONV)),
        "conv_ln_bias": nrm((L, D_CONV), 0.02),
        "pool_w": nrm((L, N_POOL_GROUPS, POOL_GROUP_DIM, POOL_GROUP_DIM), POOL_GROUP_DIM ** -0.5),
        "pool_scale": 1.0 + 0.1 * jax.random.normal(next(ks), (L, D_POOL), jnp.float32),
        "q_norm": gain((L, HEAD_DIM)),
        "k_norm": gain((L, HEAD_DIM)),
        "lambda_q1": nrm((L, HEAD_DIM), 0.1),
        "lambda_k1": nrm((L, HEAD_DIM), 0.1),
        "lambda_q2": nrm((L, HEAD_DIM), 0.1),
        "lambda_k2": nrm((L, HEAD_DIM), 0.1),
        "attn_subln": gain((L, V_DIM)),
        "w_out": nrm((L, D_MIX, D_MODEL), D_MIX ** -0.5),
        "ffn2_norm": gain((L, D_MODEL)),
        "ffn2_w_gate": nrm((L, D_MODEL, D_FF_2), D_MODEL ** -0.5),
        "ffn2_w_up": nrm((L, D_MODEL, D_FF_2), D_MODEL ** -0.5),
        "ffn2_w_down": nrm((L, D_FF_2, D_MODEL), D_FF_2 ** -0.5),
        "post_norm": gain((L, D_MODEL)),
    }

def second_block(x, ffn1_norm, ffn1_w_gate, ffn1_w_up, ffn1_w_down, mix_norm, w_in,
              conv_dw, conv_dw_bias, conv_ln_gain, conv_ln_bias, pool_w, pool_scale,
              q_norm, k_norm, lambda_q1, lambda_k1, lambda_q2, lambda_k2, attn_subln,
              w_out, ffn2_norm, ffn2_w_gate, ffn2_w_up, ffn2_w_down, post_norm):
    B_, S_ = x.shape[0], x.shape[1]
    slopes = jnp.exp2(-8.0 * jnp.arange(1, N_HEADS + 1, dtype=jnp.float32) / N_HEADS)
    for l in range(DEPTH):
        lambda_init = 0.8 - 0.6 * math.exp(-0.3 * l)
        x = x + 0.5 * swiglu_ffn_2(rms_norm(x, ffn1_norm[l]), ffn1_w_gate[l], ffn1_w_up[l], ffn1_w_down[l])
        h = rms_norm(x, mix_norm[l])
        u = h @ w_in[l]
        u_conv = u[..., :2 * D_CONV]
        u_pool = u[..., 2 * D_CONV:2 * D_CONV + D_POOL]
        q, k, v = jnp.split(u[..., 2 * D_CONV + D_POOL:], 3, axis=-1)
        y_conv = conformer_conv(u_conv, conv_dw[l], conv_dw_bias[l], conv_ln_gain[l], conv_ln_bias[l])
        y_pool = multiscale_pool(u_pool, pool_w[l], pool_scale[l])
        q = rms_norm(q.reshape(B_, S_, N_HEADS, 2, HEAD_DIM), q_norm[l]) * (HEAD_DIM ** -0.5)
        k = rms_norm(k.reshape(B_, S_, N_HEADS, 2, HEAD_DIM), k_norm[l])
        v = v.reshape(B_, S_, N_HEADS, V_DIM)
        lam = (jnp.exp(jnp.sum(lambda_q1[l].astype(jnp.float32) * lambda_k1[l].astype(jnp.float32)))
               - jnp.exp(jnp.sum(lambda_q2[l].astype(jnp.float32) * lambda_k2[l].astype(jnp.float32)))
               + lambda_init)
        o = diff_attention(q, k, v, lam, slopes)
        y_attn = (rms_norm(o, attn_subln[l]) * (1.0 - lambda_init)).reshape(B_, S_, D_ATTN)
        y = jnp.concatenate([y_conv, y_pool, y_attn.astype(y_conv.dtype)], axis=-1) @ w_out[l]
        x = x + y
        x = x + 0.5 * swiglu_ffn_2(rms_norm(x, ffn2_norm[l]), ffn2_w_gate[l], ffn2_w_up[l], ffn2_w_down[l])
        x = rms_norm(x, post_norm[l])
    return x


def setup_inputs(seed=0):
    out = dict(first_inputs(seed))
    for name, value in second_inputs(seed + 1).items():
        if name != "x":
            out[name + "_2"] = value
    return out


def reference(
    x, p, ffn1_norm, ffn1_wi, ffn1_wo, mix_norm, w_in, b_igate, b_fgate, ml_out_norm, q_norm,
    k_norm, sinks, rel_bias, w_a, w_b, w_out, ffn2_norm, ffn2_wi, ffn2_wo, ple_norm, w_ple_gate,
    w_ple, ffn1_norm_2, ffn1_w_gate_2, ffn1_w_up_2, ffn1_w_down_2, mix_norm_2, w_in_2,
    conv_dw_2, conv_dw_bias_2, conv_ln_gain_2, conv_ln_bias_2, pool_w_2, pool_scale_2, q_norm_2,
    k_norm_2, lambda_q1_2, lambda_k1_2, lambda_q2_2, lambda_k2_2, attn_subln_2, w_out_2,
    ffn2_norm_2, ffn2_w_gate_2, ffn2_w_up_2, ffn2_w_down_2, post_norm_2,
):
    x = first_block(
        x, p, ffn1_norm, ffn1_wi, ffn1_wo, mix_norm, w_in, b_igate, b_fgate, ml_out_norm,
        q_norm, k_norm, sinks, rel_bias, w_a, w_b, w_out, ffn2_norm, ffn2_wi, ffn2_wo, ple_norm,
        w_ple_gate, w_ple,
    )
    return second_block(
        x, ffn1_norm_2, ffn1_w_gate_2, ffn1_w_up_2, ffn1_w_down_2, mix_norm_2, w_in_2,
        conv_dw_2, conv_dw_bias_2, conv_ln_gain_2, conv_ln_bias_2, pool_w_2, pool_scale_2,
        q_norm_2, k_norm_2, lambda_q1_2, lambda_k1_2, lambda_q2_2, lambda_k2_2, attn_subln_2,
        w_out_2, ffn2_norm_2, ffn2_w_gate_2, ffn2_w_up_2, ffn2_w_down_2, post_norm_2,
    )


_drawn_inputs = setup_inputs


def setup_inputs(seed=0):
    import zlib

    import numpy as np

    out = dict(_drawn_inputs(seed))
    spreads = {}
    factors = {'b_igate': 64.0,
     'q_norm': 5.946,
     'k_norm': 4.553,
     'sinks': 8.0,
     'ple_norm': 3.219,
     'ffn1_norm_2': 4.734,
     'mix_norm_2': 2.669,
     'conv_dw_bias_2': 4.148,
     'conv_ln_gain_2': 7.411,
     'conv_ln_bias_2': 7.102,
     'q_norm_2': 5.892,
     'k_norm_2': 5.709,
     'lambda_q1_2': 5.548,
     'lambda_k1_2': 3.854,
     'attn_subln_2': 5.222,
     'ffn2_norm_2': 6.426}
    for name, (base, spread) in spreads.items():
        noise = np.random.default_rng([zlib.crc32(name.encode()), seed]).standard_normal(out[name].shape)
        drawn = base * np.exp(spread * noise) if base else spread * noise
        out[name] = __import__('jax').numpy.asarray(drawn.astype(out[name].dtype))
    for name, factor in factors.items():
        out[name] = (out[name] * factor).astype(out[name].dtype)
    return out
```

```python
import math
from contextlib import ExitStack

import numpy as np
import concourse.bass as bass
from concourse import mybir

F32 = mybir.dt.float32
F32R = mybir.dt.float32r
BF16 = mybir.dt.bfloat16
ALU = mybir.AluOpType
ACT = mybir.ActivationFunctionType
AXX = mybir.AxisListType.X

P = 128
D = 1024
S = 256
KD = D // P
FF = 2816
NG = FF // 256
EPS = 1e-6
UC = 1024
NEG = -1.0e30
RAW_SLOTS = 4
W_SLOTS = 5
HT_SLOTS = 4

MIX1 = [("g0", 264), ("sq", 512), ("qk", 512), ("mv", 512), ("mo", 512),
        ("ga0", 512), ("ga1", 512), ("gb0", 512), ("gb1", 512)]
MIX2 = [("conv", 512), ("q", 512), ("k", 512), ("v", 512), ("pool", 256)]
BC1 = [("oln", 512), ("sink", 8), ("gb", 8)]
BC2 = [("post", 1024), ("lam", 256)]


def spans(items):
    out, at = {}, 0
    for name, n in items:
        out[name] = (at, at + n)
        at += n
    return out, at


def ffn_order():
    order = [("gu", 0)]
    for g in range(1, NG):
        order += [("gu", g), ("o", g - 1)]
    return order + [("o", NG - 1)]


class Line:

    def __init__(self, sem, serial=False):
        self.sem, self.n, self.prog, self.passed, self.serial = sem, 0, [], {}, serial

    def put(self, call, after=(), inc=True, signal=None):
        need = {}
        if self.serial and self.n:
            after = [after, (self.sem, self.n)]
        for sem, value in flat(after):
            if self.passed.get(sem.name, 0) < value:
                self.passed[sem.name] = value
                need[sem.name] = (sem, value)
        if signal is None and inc:
            self.n += 1
            signal = (self.sem, 1)
        self.prog.append((list(need.values()), call, signal))
        return (self.sem, self.n)

    def run(self, eng):
        for waits, call, signal in self.prog:
            for sem, value in waits:
                eng.wait_ge(sem, value)
            ins = call(eng)
            if signal is not None:
                ins.then_inc(signal[0], signal[1])


def flat(after):
    for x in after:
        if not x:
            continue
        if isinstance(x, tuple):
            yield x
        else:
            yield from flat(x)


def program(nc, d, out):
    ctx = ExitStack()
    with ctx:
        def sb(name, shape, dt=F32):
            return ctx.enter_context(nc.sbuf_tensor(name, shape, dt))

        def sem(name):
            return ctx.enter_context(nc.semaphore(name))

        PE, VE, SE, SP = (Line(sem("s_" + n)) for n in ("pe", "dve", "act", "sp"))
        PO = Line(sem("s_pool"), serial=True)

        raw = [sb(f"raw{i}", [P, UC]) for i in range(RAW_SLOTS)]
        whi = [sb(f"whi{i}", [P, UC], F32R) for i in range(W_SLOTS)]
        wlo = [sb(f"wlo{i}", [P, UC], F32R) for i in range(W_SLOTS)]
        HTh = sb("HTh", [P, 2 * HT_SLOTS, S], F32R)
        HTl = sb("HTl", [P, 2 * HT_SLOTS, S], F32R)
        XTh = sb("XTh", [P, KD, S], F32R)
        XTl = sb("XTl", [P, KD, S], F32R)
        X = sb("X", [P, 2, D])
        junk = sb("junk", [P, D], BF16)
        sbuf_s = sb("sbuf_s", [P, 2, 2, 256])
        sbuf_h = sb("sbuf_h", [P, 2, 2, 256])
        ident = sb("ident", [P, P])
        st = sb("st", [P, 2, 400])
        cst = sb("cst", [P, 4])
        gcol = sb("gcol", [P, 14 * KD])
        hcol = sb("hcol", [P, 22])
        pcol = sb("pcol", [P, KD])
        postc = sb("postc", [P, KD])
        pb = [ctx.enter_context(nc.psum_tensor(f"pb{i}", [P, 512], F32)) for i in range(8)]

        bank_free = [[] for _ in range(8)]

        def mm(o, l, r, start, stop, after=(), inc=False):
            return PE.put(lambda e: e.matmul(o, l, r, start=start, stop=stop), after, inc)

        def tr(o, i, after=(), inc=False):
            n = i.shape[0]
            return PE.put(lambda e: e.transpose(o, i, ident[0:n, 0:n]), after, inc)

        def act(o, i, f, after=(), scale=1.0, bias=None, acc=None):
            kw = {"scale": scale}
            if bias is not None:
                kw["bias"] = bias
            if acc is not None:
                kw["accum_out"] = acc
            return SE.put(lambda e: e.activation(o, i, f, **kw), after)

        def tt(o, a, b, op, after=()):
            return VE.put(lambda e: e.tensor_tensor(o, a, b, op), after)

        def stt(o, a, s, b, op0, op1, after=()):
            return VE.put(lambda e: e.scalar_tensor_tensor(out=o, in0=a, scalar=s, in1=b, op0=op0, op1=op1), after)

        def ts(o, a, s1, s2, op0, op1=None, after=()):
            if op1 is None:
                return VE.put(lambda e: e.tensor_scalar(o, a, s1, None, op0), after)
            return VE.put(lambda e: e.tensor_scalar(o, a, s1, s2, op0, op1), after)

        def cp(o, i, after=()):
            return VE.put(lambda e: e.tensor_copy(o, i), after)

        def red(o, i, op, after=()):
            return VE.put(lambda e: e.tensor_reduce(o, i, AXX, op), after)

        def recip(o, i, after=()):
            return VE.put(lambda e: e.reciprocal(o, i), after)

        def p_ts(o, a, s1, s2, op0, op1, after=()):
            return PO.put(lambda e: e.tensor_scalar(o, a, s1, s2, op0, op1), after)

        def p_pow(o, a, b, after=()):
            return PO.put(lambda e: e.tensor_tensor(o, a, b, ALU.pow), after)

        def load(line, dst, src, after=()):
            s = sem(f"s_ld{len(loads)}")
            loads.append(s)
            line.put(lambda e: e.dma_start(dst, src), after, signal=(s, 16))
            return (s, 16)

        loads = []

        units = d["cols"]
        n_units = len(units)
        raw_sem = [sem(f"s_raw{i}") for i in range(RAW_SLOTS)]
        dma_tok, split_tok, freed = {}, {}, {}
        at = {"dma": 0, "split": 0, "use": 0}

        def stream_dma(to):
            while at["dma"] < min(to, n_units) and at["dma"] - RAW_SLOTS < at["split"]:
                u = at["dma"]
                c = units[u]
                dst, src = raw[u % RAW_SLOTS][:, 0:c], d["W"][u, :, 0:c]
                after = split_tok[u - RAW_SLOTS] if u >= RAW_SLOTS else ()
                SP.put(lambda e, dst=dst, src=src: e.dma_start(dst, src), after,
                       signal=(raw_sem[u % RAW_SLOTS], 16))
                dma_tok[u] = (raw_sem[u % RAW_SLOTS], 16 * (u // RAW_SLOTS + 1))
                at["dma"] += 1

        def stream_split(to):
            while at["split"] < min(to, n_units):
                u = at["split"]
                if u >= W_SLOTS and u - W_SLOTS not in freed:
                    return
                stream_dma(u + 1)
                c = units[u]
                r, h, l = raw[u % RAW_SLOTS][:, 0:c], whi[u % W_SLOTS][:, 0:c], wlo[u % W_SLOTS][:, 0:c]
                slot = freed.get(u - W_SLOTS)
                th = act(h, r, ACT.Copy, [dma_tok[u], slot])
                tl = tt(l, r, h.bitcast(F32), ALU.subtract, [dma_tok[u], slot, th])
                split_tok[u] = [th, tl]
                at["split"] += 1
                stream_dma(u + 1 + RAW_SLOTS)

        def next_unit():
            u = at["use"]
            at["use"] += 1
            stream_split(u + W_SLOTS - 1)
            for _ in range(min(state["bg_n"], len(state["bg"]))):
                state["bg"].pop(0)()
            assert at["split"] > u
            return u, whi[u % W_SLOTS], wlo[u % W_SLOTS], split_tok[u]

        def product(lh, ll, chunks, ready, ncols, kper, banks, begin=True, end=True):
            done = {}
            nk = len(chunks)
            for k0 in range(0, nk, kper):
                u, h, l, got = next_unit()
                jobs = [(t, b) for b in range(len(banks[0])) for t in range(2)]
                for j, (t, b) in enumerate(jobs):
                    bank, c0, n = banks[t][b]
                    for k in range(k0, k0 + kper):
                        c = chunks[k]
                        wc = (k - k0) * ncols + c0
                        o = pb[bank][:, 0:n]
                        ah, al = lh[:, c, t * P:(t + 1) * P], ll[:, c, t * P:(t + 1) * P]
                        bh, bl = h[:, wc:wc + n], l[:, wc:wc + n]
                        first, last = begin and k == 0, end and k == nk - 1
                        mm(o, ah, bh, first, False, [got, ready(c, t), bank_free[bank] if first else ()])
                        mm(o, ah, bl, False, False)
                        fin = j == len(jobs) - 1 and k == k0 + kper - 1
                        tok = mm(o, al, bh, False, last, inc=last or fin)
                        if last:
                            done[(t, b)] = tok
                        if fin:
                            freed[u] = tok
                if k0 + kper >= 2:
                    run_later()
            return done

        small = {"set": 0, "at": 0}

        def col(n):
            a = st[:, small["set"], small["at"]:small["at"] + n]
            small["at"] += n
            assert small["at"] <= 400
            return a

        def new_layer():
            small["set"] ^= 1
            small["at"] = 0

        def rstd(ss, n, count, after, extra=None):
            v, r = col(n), col(n)
            a = p_ts(v, ss, 1.0 / count, EPS, ALU.mult, ALU.add, after)
            a = p_pow(r, v, cst[:, 0:1].to_broadcast([P, n]), [a, t_cst])
            if extra is not None:
                r2 = col(n)
                a = p_ts(r2, r, extra, 0.0, ALU.mult, ALU.add, [a])
                r = r2
            return r, a

        t_id = load(SP, ident[:, :], d["ident"])
        t_xs = [load(SE, X[:, t, :], d["x"][:, t, :]) for t in range(2)]
        t_gcol = load(SP, gcol[:, :], d["gcol"])
        t_hcol = load(PO, hcol[:, :], d["hcol"])
        t_cst = PO.put(lambda e: e.memset(cst[:, :], -0.5))
        x_tok = {(t, n): [t_xs[t]] for t in range(2) for n in range(2)}
        state = {"xt_free": [], "junk": [], "later": None, "bg": [], "bg_n": 0}

        def run_later():
            if state["later"] is not None:
                call, state["later"] = state["later"], None
                call()

        OB = [[0, 1], [2, 3]]
        WIDE = [[(OB[t][n], n * 512, 512) for n in range(2)] for t in range(2)]
        WIDE4 = [[(4 + OB[t][n], n * 512, 512) for n in range(2)] for t in range(2)]

        def turn_chunk(toks, c, src, tok, bank, gain=None, gain_tok=None):
            for t in range(2):
                k = tr(pb[bank][:, t * P:(t + 1) * P], src(t), [tok(t), bank_free[bank], t_id], inc=(t == 1))
            o = pb[bank][:, 0:S]
            th = act(XTh[:, c, :], o, ACT.Copy, [k, state["xt_free"], gain_tok], scale=1.0 if gain is None else gain)

            def low():
                hi = XTh[:, c, :].bitcast(F32)
                if gain is None:
                    tl = tt(XTl[:, c, :], o, hi, ALU.subtract, [k, th])
                else:
                    tl = stt(XTl[:, c, :], o, gain, hi, ALU.mult, ALU.subtract, [k, th])
                bank_free[bank] = [tl]
                toks[c] = [th, tl]
                state["xt_read"] = k
            return low

        def square_sum(ss):
            for t in range(2):
                a = act(junk[:, :], X[:, t, :], ACT.Square, [x_tok[(t, 0)], x_tok[(t, 1)], state["junk"]],
                        acc=ss[:, t:t + 1])
                state["junk"] = [a]
            return a

        TO_FFN = [4, 5, 6, 7, 6, 7, 6, 7]
        TO_MIX = [4, 5, 6, 7, 4, 5, 6, 7]
        AFTER_GATE = [0, 1, 2, 3, 0, 1, 2, 3]

        class Norm:

            def __init__(self, which, banks, gains=None, gains_tok=None):
                self.toks, self.r, self.r_tok, self.banks = {}, None, None, banks
                self.gains = gcol[:, which * KD:(which + 1) * KD] if gains is None else gains
                self.gains_tok = t_gcol if gains is None else gains_tok

            def ready(self, c, t):
                return self.toks[c]

            def chunks(self, lo, hi):
                return [turn_chunk(self.toks, c, lambda t: X[:, t, c * P:(c + 1) * P], lambda t: x_tok[(t, c // 4)],
                                   self.banks[c], self.gains[:, c:c + 1], self.gains_tok) for c in range(lo, hi)]

            def rest(self):
                for c in range(4, 8):
                    self.chunks(c, c + 1)[0]()
                ss = col(2)
                a = square_sum(ss)
                self.r, self.r_tok = rstd(ss, 2, D, [a])
                state["x_read"] = [a, state["xt_read"]]

        class NormTwice(Norm):

            def rest(self):
                for c in range(4, 8):
                    self.chunks(c, c + 1)[0]()
                turned = state["xt_read"]
                s1, s2, both = col(2), col(2), col(2)
                a = square_sum(s1)
                r1, p1 = rstd(s1, 2, D, [a])
                for t in range(2):
                    v = stt(X[:, t, :], X[:, t, :], r1[:, t:t + 1], state["post_gain"], ALU.mult, ALU.mult,
                            [p1, turned, state["post_tok"]])
                    x_tok[(t, 0)] = x_tok[(t, 1)] = [v]
                a = square_sum(s2)
                r2, p2 = rstd(s2, 2, D, [a])
                self.r, self.r_tok = both, PO.put(lambda e: e.tensor_tensor(both, r1, r2, ALU.mult), [p1, p2])
                state["x_read"] = [a, turned]

        def tail_product(lh, ll, chunks, ready, banks, begin, half, between):
            if len(chunks) > 2:
                product(lh, ll, chunks[:-2], ready, 1024, 1, banks, begin=begin, end=False)
                begin = False
                if lh is XTh:
                    state["xt_free"] = [freed[at["use"] - 1]]
            two = [next_unit(), next_unit()]
            for n in range(2):
                done = {}
                for t in range(2):
                    bank, c0, w = banks[t][n]
                    o = pb[bank][:, 0:w]
                    if n == 1 and t == 1:
                        between()
                    for i, (c, (u, h, l, got)) in enumerate(zip(chunks[-2:], two)):
                        ah, al = lh[:, c, t * P:(t + 1) * P], ll[:, c, t * P:(t + 1) * P]
                        first = begin and i == 0
                        mm(o, ah, h[:, c0:c0 + w], first, False, [got, ready(c, t), bank_free[bank] if first else ()])
                        mm(o, ah, l[:, c0:c0 + w], False, False)
                        tok = mm(o, al, h[:, c0:c0 + w], False, i == 1, inc=(i == 1))
                    done[t] = tok
                half(n, done)
            for u, _, _, _ in two:
                freed[u] = tok
            return tok

        def into_x(lh, ll, chunks, ready, factor, norm, begin=True):
            lows = []

            def half(n, done):
                for t in range(2):
                    xs = X[:, t, n * 512:(n + 1) * 512]
                    b = OB[t][n]
                    tok = stt(xs, pb[b][:, :], factor, xs, ALU.mult, ALU.add, [done[t], state["x_read"]])
                    bank_free[b] = [tok]
                    x_tok[(t, n)] = [tok]
                    if n == 1:
                        for low in lows[2 * t:2 * t + 2]:
                            low()

            def between():
                if norm is not None:
                    lows.extend(norm.chunks(0, 4))
                    for _ in range(2):
                        lows.pop(0)()
                    lows[:0] = [lambda: None] * 2

            tok = tail_product(lh, ll, chunks, ready, WIDE, begin, half, between)
            if norm is not None:
                state["later"] = norm.rest
            return tok

        ht_free = [[] for _ in range(HT_SLOTS)]
        ht_tok = {}
        sh = {"s": [[], []], "h": [[], []]}

        def ffn(norm, following, mid=None):
            h_tok = {}

            def gate_up(g):
                q = g % 2
                b0 = 4 + 2 * q
                banks = [[(b0 + t, 0, 512)] for t in range(2)]
                done = product_gu(g, banks)
                toks = []
                for t in range(2):
                    b = pb[b0 + t]
                    a = act(sbuf_s[:, q, t, :], b[:, 0:256], ACT.Silu, [done[t], norm.r_tok, sh["s"][q]],
                            scale=norm.r[:, t:t + 1])
                    v = stt(sbuf_h[:, q, t, :], b[:, 256:512], norm.r[:, t:t + 1], sbuf_s[:, q, t, :],
                            ALU.mult, ALU.mult, [a, sh["h"][q]])
                    bank_free[b0 + t] = [v]
                    toks.append(v)
                sh["s"][q] = toks
                h_tok[g] = toks

            def product_gu(g, banks):
                done = {}
                for i in range(4):
                    if i == 2 and g >= 1:
                        turn(g - 1)
                    u, h, l, got = next_unit()
                    for t in range(2):
                        bank = banks[t][0][0]
                        o = pb[bank][:, :]
                        for k in (2 * i, 2 * i + 1):
                            ah, al = XTh[:, k, t * P:(t + 1) * P], XTl[:, k, t * P:(t + 1) * P]
                            w0 = (k % 2) * 512
                            mm(o, ah, h[:, w0:w0 + 512], k == 0, False,
                               [got, norm.ready(k, t), bank_free[bank] if k == 0 else ()])
                            mm(o, ah, l[:, w0:w0 + 512], False, False)
                            last = k == KD - 1
                            fin = t == 1 and k % 2 == 1
                            tok = mm(o, al, h[:, w0:w0 + 512], False, last, inc=last or fin)
                            if last:
                                done[t] = tok
                            if fin:
                                freed[u] = tok
                                state["xt_free"] = [tok]
                    if i == 0:
                        run_later()
                return done

            def turn(g):
                q, slot = g % 2, g % HT_SLOTS
                bank = 4 + 2 * q
                for k in range(2):
                    for t in range(2):
                        p = tr(pb[bank][:, k * S + t * P:k * S + (t + 1) * P], sbuf_h[:, q, t, k * P:(k + 1) * P],
                               [h_tok[g], bank_free[bank]], inc=(k == 1 and t == 1))
                sh["h"][q] = [p]
                hh = HTh[:, 2 * slot:2 * slot + 2, :].rearrange("p k t -> p (k t)")
                hl = HTl[:, 2 * slot:2 * slot + 2, :].rearrange("p k t -> p (k t)")
                th = act(hh, pb[bank][:, :], ACT.Copy, [p, ht_free[slot]])
                tl = tt(hl, pb[bank][:, :], hh.bitcast(F32), ALU.subtract, [p, th, ht_free[slot]])
                bank_free[bank] = [tl]
                ht_tok[slot] = [th, tl]

            def down(g):
                slot = g % HT_SLOTS
                chunks = [2 * slot, 2 * slot + 1]
                if g == NG - 1:
                    into_x(HTh, HTl, chunks, lambda c, t: ht_tok[slot], 0.5, following, begin=False)
                else:
                    product(HTh, HTl, chunks, lambda c, t: ht_tok[slot], 1024, 1, WIDE, begin=(g == 0), end=False)
                ht_free[slot] = [freed[at["use"] - 1]]

            for kind, g in ffn_order():
                if kind == "gu":
                    gate_up(g)
                    if g == 2 and mid is not None:
                        mid()
                else:
                    if g == NG - 1:
                        turn(g)
                    down(g)

        t_ident_small = t_id
        c1, n1 = spans([("tri", 512), ("eye", 512), ("cmask", 256), ("sel", 512), ("bc", 528), ("bias", 2048),
                        ("sq", 1024), ("sqT", 1024), ("kT", 512), ("qk", 1024), ("qkT", 1024),
                        ("vx", 1032), ("E", 1536), ("pr", 3072), ("prT", 3072), ("mo", 1024), ("gab", 4096),
                        ("rows", 512)])
        bc1, _ = spans(BC1)
        bc2, _ = spans(BC2)
        first = ExitStack()
        scr = first.enter_context(nc.sbuf_tensor("scr1", [P, n1], F32))
        PTh = first.enter_context(nc.sbuf_tensor("PTh", [P, 2, S], F32R))
        PTl = first.enter_context(nc.sbuf_tensor("PTl", [P, 2, S], F32R))

        def part(name, **kw):
            a = scr[:, c1[name][0]:c1[name][1]]
            return a.rearrange(kw["form"], **{k: v for k, v in kw.items() if k != "form"}) if kw else a

        tri = part("tri", form="p (s t) -> p s t", s=2)
        eye = part("eye", form="p (s t) -> p s t", s=2)
        cmask = part("cmask")
        sel = part("sel", form="p (h m) -> p h m", h=4)
        bias = part("bias", form="p (h j) -> p h j", h=8)

        def bcp1(name):
            return part("bc")[:, bc1[name][0]:bc1[name][1]]

        t_tri = load(PO, tri, d["tri"])
        t_eye = load(PO, eye, d["eye"])
        t_cm = load(PO, cmask, d["cmask"])
        t_sel = load(PO, sel[0:4, :, :], d["sel"])

        stage = part("pr", form="p (h n) -> p h n", h=8)
        rbT = part("prT")[:, 0:1024].rearrange("p (h m) -> p h m", h=8)
        oh = part("prT")[:, 1024:1408]
        t_rb1 = PO.put(lambda e: e.memset(rbT[32:33, :, :], 1.0))
        t_rb = load(PO, rbT[0:32, :, :], d["rb"])
        t_oh = load(PO, oh[0:33, :], d["onehot"])
        s_bo = sem("s_bo")
        skew = bass.AP(d["scratch"].tensor, 0, [[383, P], [384 * P, 8], [1, 256]])

        def bias_table():
            for h in range(8):
                b = 4 + h % 4
                k = mm(pb[b][:, 0:384], rbT[0:33, h, :], oh[0:33, :], True, True, [t_rb1, t_rb, t_oh, bank_free[b]],
                       inc=True)
                v = cp(stage[:, h, :], pb[b][:, 0:384], [k])
                bank_free[b] = [v]
            PO.put(lambda e: e.dma_start(d["scratch"].rearrange("h p n -> p h n"), stage), [v], signal=(s_bo, 16))
            state["t_bias"] = load(PO, bias, skew, [(s_bo, 16)])
            state["pr_free"] = [(s_bo, 16), v]

        state["pr_free"] = []
        state["free1"] = []

        def small_inputs1(layer):
            state["t_bc1"] = load(PO, part("bc"), d["bc1"][layer:layer + 1, :].to_broadcast([P, 528]), state["free1"])

        def headed(a, n):
            return a.rearrange("p (h e) -> p h e", h=n)

        def head_norm(b0, done, norm, dst, buf, extra, wait, T, key):
            T[key] = []
            for t in range(2):
                src = pb[b0 + t][:, :]
                ss = col(8)
                a = act(buf[:, t, :], src, ACT.Square, [done[(t, 0)], norm.r_tok, wait], scale=norm.r[:, t:t + 1])
                v = red(ss, headed(buf[:, t, :], 8), ALU.add, [a])
                rr, p = rstd(ss, 8, 64, [v])
                r2 = col(8)
                p = p_ts(r2, rr, norm.r[:, t:t + 1], extra, ALU.mult, ALU.mult, [p, norm.r_tok])
                w = tt(headed(dst[:, t, :], 8), headed(src, 8), r2.unsqueeze(2).to_broadcast([P, 8, 64]), ALU.mult,
                       [p, a, wait])
                bank_free[b0 + t] = [w]
                T[key].append(w)

        def mixer1(layer, norm, following):
            ready = norm.ready
            fr = state["free1"]
            t_bc = state["t_bc1"]
            gq, gk = (hcol[:, 2 * layer + i:2 * layer + i + 1] for i in range(2))
            sq = part("sq", form="p (t n) -> p t n", t=2)
            sk = sbuf_h[:, 0, :, 0:128]
            sv = sbuf_h[:, 0, :, 128:256]
            kd = sbuf_h[:, 1, :, :].rearrange("p t (g u e) -> p t g u e", g=2, u=2)
            tmp = sbuf_s[:, :, :, :].rearrange("p a b c -> p (a b c)").rearrange("p (t n) -> p t n", t=2)
            sqT = part("sqT", form="p (c t) -> p c t", c=4)
            kT = part("kT", form="p (g t) -> p g t", g=2)
            qk = part("qk", form="p (t n) -> p t n", t=2)
            qkT = part("qkT", form="p (c t) -> p c t", c=4)
            vx = part("vx", form="p (t h e) -> p t h e", t=2, h=4)
            E = part("E", form="p (h n) -> p h n", h=4)
            pr0 = part("pr")[:, 0:1024].rearrange("p (h j) -> p h j", h=8)
            pr1 = part("pr")[:, 1024:3072].rearrange("p (h j) -> p h j", h=8)
            pt0 = part("prT")[:, 0:1024].rearrange("p (h j) -> p h j", h=8)
            pt1 = part("prT")[:, 1024:3072].rearrange("p (h s j) -> p h s j", h=8, s=2)
            mo = part("mo", form="p (t n) -> p t n", t=2)
            gab = part("gab", form="p (w t n) -> p w t n", w=2, t=2)
            arow = part("rows")[0:4, 0:256]
            mrow = part("rows")[0:4, 256:512]
            gz = col(16).rearrange("p (t n) -> p t n", t=2)
            T = {}
            turn_bank = {"n": 0}
            pair = {"n": 0}

            def chain_bank():
                turn_bank["n"] += 1
                return 4 + (turn_bank["n"] - 1) % 4

            def group(ncols):
                b0 = 2 * (pair["n"] % 2)
                pair["n"] += 1
                banks = [[(b0 + t, 0, ncols)] for t in range(2)]
                done = product(XTh, XTl, list(range(KD)), ready, ncols, 2, banks)
                state["xt_free"] = [done[(1, 0)]]
                return b0, done

            def g_small():
                b0, done = group(264)
                T["gz"], T["skv"] = [], []
                r, r_tok = norm.r, norm.r_tok
                for t in range(2):
                    b = pb[b0 + t]
                    v = stt(gz[:, t, :], b[:, 0:8], r[:, t:t + 1], bcp1("gb"), ALU.mult, ALU.add,
                            [done[(t, 0)], r_tok, t_bc])
                    a = act(sbuf_h[:, 0, t, :], b[:, 8:264], ACT.Copy, [v, sh["h"]], scale=r[:, t:t + 1])
                    bank_free[b0 + t] = [a]
                    T["gz"].append(v)
                    T["skv"].append(a)

            def g_copy(dst, key, form=None, on_act=True):
                b0, done = group(512)
                r, r_tok = norm.r, norm.r_tok
                T[key] = []
                for t in range(2):
                    src = pb[b0 + t][:, :]
                    if form is not None:
                        src = src.rearrange(form, h=4)
                    if on_act:
                        a = act(dst(t), src, ACT.Copy, [done[(t, 0)], r_tok, fr], scale=r[:, t:t + 1])
                    else:
                        a = ts(dst(t), src, r[:, t:t + 1], None, ALU.mult, after=[done[(t, 0)], r_tok, fr])
                    bank_free[b0 + t] = [a]
                    T[key].append(a)

            def gates_a():
                f = gz[:, :, 4:8]
                e1, mx, nlf = (col(8).rearrange("p (t n) -> p t n", t=2) for _ in range(3))
                a = act(e1, f, ACT.Abs, [T["gz"]])
                a = act(e1, e1, ACT.Exp, [a], scale=-1.0)
                m = ts(mx, f, -1.0, 0.0, ALU.mult, ALU.max, [T["gz"]])
                v = ts(e1, e1, 1.0, None, ALU.add, after=[a])
                a = act(e1, e1, ACT.Ln, [v])
                T["nlf"] = [tt(nlf, e1, mx, ALU.add, [a, m])]
                T["nlf_ap"] = nlf

            def gates_b():
                nlf = T["nlf_ap"]
                b = chain_bank()
                o = pb[b][0:4, 0:256]
                w = [T["nlf"], T["gz"], t_tri, t_eye, bank_free[b]]
                for s in range(2):
                    mm(o, gz[:, s, 0:4], eye[:, s, :], s == 0, False, w)
                for s in range(2):
                    k = mm(o, nlf[:, s, :], tri[:, s, :], False, s == 1, inc=(s == 1))
                v = cp(arow, o, [k, fr])
                bank_free[b] = [v]
                T["arow"] = v
                T["mrow"] = VE.put(lambda e: e.tensor_tensor_scan(mrow, arow, arow, 0.0, ALU.max, ALU.max), [v])

            def gates_c():
                nlf = T["nlf_ap"]
                b = chain_bank()
                for t in range(2):
                    for s in range(2):
                        mm(pb[b][:, 4 * t:4 * t + 4], tri[:, s, t * P:(t + 1) * P], nlf[:, s, :], s == 0, s == 1,
                           [T["arow"], T["mrow"], bank_free[b], T["nlf"]])
                for i, row in enumerate((arow, mrow)):
                    for t in range(2):
                        k = tr(pb[b][:, 8 + 8 * i + 4 * t:12 + 8 * i + 4 * t], row[:, t * P:(t + 1) * P],
                               inc=(i == 1 and t == 1))
                tk = col(24)
                v = cp(tk, pb[b][:, 0:24], [k])
                bank_free[b] = [v]
                em = col(8)
                w = tt(em, tk[:, 0:8], tk[:, 16:24], ALU.subtract, [v])
                T["em"] = act(em, em, ACT.Exp, [w])
                T["em_ap"] = em
                T["a_ap"] = tk[:, 8:16]
                T["tk"] = v

            def g_query():
                b0, done = group(512)
                head_norm(b0, done, norm, sq, tmp, 0.125, [sh["s"], fr], T, "sq2")

            def key_norm():
                a = act(tmp[:, :, 0:128], sk, ACT.Square, [T["skv"], T["sq2"]])
                ssk = col(4)
                v2 = red(ssk.rearrange("p (t g) -> p t g", t=2),
                         tmp[:, :, 0:128].rearrange("p t (g e) -> p t g e", e=64), ALU.add, [a])
                rk, p2 = rstd(ssk, 4, 64, [v2])
                T["kd"] = []
                for t in range(2):
                    k3 = headed(sk[:, t, :], 2)
                    for u in range(2):
                        w = tt(kd[:, t, :, u, :], k3, rk[:, 2 * t:2 * t + 2].unsqueeze(2).to_broadcast([P, 2, 64]),
                               ALU.mult, [p2, sh["h"]])
                    T["kd"].append(w)

            def sw_turn():
                b = chain_bank()
                for g in range(2):
                    for t in range(2):
                        k = tr(pb[b][:, g * S + t * P:g * S + (t + 1) * P],
                               kd[:, t, g, :, :].rearrange("p u e -> p (u e)"), [T["kd"], bank_free[b]],
                               inc=(g == 1 and t == 1))
                v = act(kT.rearrange("p g t -> p (g t)"), pb[b][:, :], ACT.Copy, [k, fr, t_hcol], scale=gk)
                bank_free[b] = [v]
                T["kT"] = v
                T["sqT"] = []
                for c0 in (0, 2):
                    b = chain_bank()
                    for c in (c0, c0 + 1):
                        for t in range(2):
                            k = tr(pb[b][:, (c - c0) * S + t * P:(c - c0) * S + (t + 1) * P],
                                   sq[:, t, c * P:(c + 1) * P], [T["sq2"], bank_free[b]],
                                   inc=(c == c0 + 1 and t == 1))
                    v = act(sqT[:, c0:c0 + 2, :].rearrange("p c t -> p (c t)"), pb[b][:, :], ACT.Copy, [k, fr, t_hcol],
                            scale=gq)
                    bank_free[b] = [v]
                    T["sqT"].append(v)
                T["sq_read"] = k

            def logits(t):
                nk, j0 = (P, P) if t == 0 else (2 * P, 0)
                pr = pr0 if t == 0 else pr1
                per = 512 // nk
                T[("lg", t)] = []
                for par in range(2):
                    for i0 in range(0, 4, per):
                        b = chain_bank()
                        rows = slice(64 * par, 64 * par + 64)
                        for i in range(i0, i0 + per):
                            g = (2 * i + par) // 4
                            k = mm(pb[b][:, (i - i0) * nk:(i - i0 + 1) * nk], sqT[rows, i, t * P:(t + 1) * P],
                                   kT[rows, g, 0:nk], True, True, [T["kT"], T["sqT"], bank_free[b]],
                                   inc=(i == i0 + per - 1))
                        h0 = 4 * par + i0
                        v = tt(pr[:, h0:h0 + per, :], pb[b][:, :].rearrange("p (h j) -> p h j", h=per),
                               bias[:, h0:h0 + per, j0:256], ALU.add, [k, state["t_bias"], state["pr_free"]])
                        bank_free[b] = [v]
                        T[("lg", t)].append(v)

            def soft(t):
                pr = pr0 if t == 0 else pr1
                m, nm, den, es, rec = (col(8) for _ in range(5))
                v = red(m, pr, ALU.max, [T[("lg", t)]])
                v = tt(m, m, bcp1("sink"), ALU.max, [v, t_bc])
                n = ts(nm, m, -1.0, None, ALU.mult, after=[v])
                v = tt(es, bcp1("sink"), m, ALU.subtract, [v])
                es_t = act(es, es, ACT.Exp, [v])
                for h in range(8):
                    a = act(pr[:, h, :], pr[:, h, :], ACT.Exp, [n], bias=nm[:, h:h + 1], acc=den[:, h:h + 1])
                v = tt(den, den, es, ALU.add, [a, es_t])
                T[("rec", t)] = recip(rec, den, [v])
                T[("rec_ap", t)] = rec
                T[("pr", t)] = a

            def p_turn(t):
                pr = pr0 if t == 0 else pr1
                T[("pt", t)] = []
                if t == 0:
                    sets = [[(h, 0) for h in range(h0, h0 + 4)] for h0 in (0, 4)]
                    flatT = pt0.rearrange("p h j -> p (h j)")
                else:
                    sets = [[(h, s) for h in (h0, h0 + 1) for s in range(2)] for h0 in (0, 2, 4, 6)]
                    flatT = pt1.rearrange("p h s j -> p (h s j)")
                for n, pieces in enumerate(sets):
                    b = chain_bank()
                    for i, (h, s) in enumerate(pieces):
                        k = tr(pb[b][:, i * P:(i + 1) * P], pr[:, h, s * P:(s + 1) * P],
                               [T[("pr", t)], bank_free[b]], inc=(i == 3))
                    o = flatT[:, n * 512:(n + 1) * 512]
                    if n % 2:
                        v = act(o, pb[b][:, :], ACT.Copy, [k, fr])
                    else:
                        v = cp(o, pb[b][:, :], [k, fr])
                    bank_free[b] = [v]
                    T[("pt", t)].append(v)
                state["pr_free"] = [k]

            def attend(t):
                b = chain_bank()
                for h in range(8):
                    i, par = h % 4, h // 4
                    g = (2 * i + par) // 4
                    o = pb[b][:, (2 * i + par) * 64:(2 * i + par + 1) * 64]
                    ns = 1 if t == 0 else 2
                    for s in range(ns):
                        l = pt0[:, h, :] if t == 0 else pt1[:, h, s, :]
                        k = mm(o, l, sv[:, s, g * 64:(g + 1) * 64], s == 0, s == ns - 1,
                               [T[("pt", t)], T["skv"], bank_free[b]], inc=(h == 7 and s == ns - 1))
                o4 = sq[:, t, :].rearrange("p (i a e) -> p i a e", i=4, a=2)
                src = pb[b][:, :].rearrange("p (i a e) -> p i a e", i=4, a=2)
                rec = T[("rec_ap", t)].rearrange("p (a i) -> p i a", a=2)
                w = [k, T[("rec", t)], T["sq_read"]]
                for par in range(2):
                    v = tt(o4[:, :, par, :], src[:, :, par, :], rec[:, :, par].unsqueeze(2).to_broadcast([P, 4, 64]),
                           ALU.mult, w)
                bank_free[b] = [v]
                T[("hB", t)] = v

            def qk_turn():
                T["qkT"] = []
                for c0 in (0, 2):
                    b = chain_bank()
                    for c in (c0, c0 + 1):
                        for t in range(2):
                            k = tr(pb[b][:, (c - c0) * S + t * P:(c - c0) * S + (t + 1) * P],
                                   qk[:, t, c * P:(c + 1) * P], [T["qk"], bank_free[b]],
                                   inc=(c == c0 + 1 and t == 1))
                    v = act(qkT[:, c0:c0 + 2, :].rearrange("p c t -> p (c t)"), pb[b][:, :], ACT.Copy, [k, fr],
                            scale=(1.0 if c0 == 0 else 0.125))
                    bank_free[b] = [v]
                    T["qkT"].append(v)
                T["qk_read"] = k

            def decay():
                A = T["a_ap"]
                for h0 in (0, 2):
                    b = chain_bank()
                    for h in (h0, h0 + 1):
                        k = mm(pb[b][:, (h - h0) * S:(h - h0 + 1) * S], sel[0:4, h, :], mrow, True, True,
                               [T["mrow"], t_sel, bank_free[b]], inc=(h == h0 + 1))
                    for h in (h0, h0 + 1):
                        m = pb[b][:, (h - h0) * S:(h - h0 + 1) * S]
                        stt(E[:, h, 0:256], m, A[:, h:h + 1], cmask, ALU.subtract, ALU.max, [k, T["tk"], t_cm, fr])
                        v = stt(E[:, h, 256:384], m[:, P:2 * P], A[:, 4 + h:5 + h], cmask[:, 0:P], ALU.subtract,
                                ALU.max)
                    bank_free[b] = [v]
                T["E"] = act(E, E, ACT.Exp, [v], scale=-1.0)

            def scores():
                T["Wt"] = []
                for h in range(4):
                    b = chain_bank()
                    rows = slice(64 * (h % 2), 64 * (h % 2) + 64)
                    q, kk = qkT[rows, h // 2, :], qkT[rows, 2 + h // 2, :]
                    mm(pb[b][:, 0:256], kk[:, 0:P], q, True, True, [T["qkT"], bank_free[b]])
                    k = mm(pb[b][:, 256:384], kk[:, P:2 * P], q[:, P:2 * P], True, True, inc=True)
                    v = tt(E[:, h, :], E[:, h, :], pb[b][:, 0:384], ALU.mult, [k, T["E"]])
                    bank_free[b] = [v]
                    T["Wt"].append(v)

            def recall():
                T["hA"] = []
                rec = col(8)
                dn = col(8)
                for t in range(2):
                    for h0 in (0, 2):
                        b = chain_bank()
                        for h in (h0, h0 + 1):
                            o = pb[b][:, (h - h0) * 129:(h - h0) * 129 + 129]
                            w = [T["Wt"], T["mv"], T["ones"], bank_free[b]]
                            k = mm(o, E[:, h, t * P:(t + 1) * P], vx[:, 0, h, :], True, t == 0, w,
                                   inc=(t == 0 and h == h0 + 1))
                            if t == 1:
                                k = mm(o, E[:, h, 256:384], vx[:, 1, h, :], False, True, inc=(h == h0 + 1))
                        n = pb[b][:, 0:258].rearrange("p (h e) -> p h e", h=2)
                        i = 4 * t + h0
                        d2 = dn[:, i:i + 2].unsqueeze(2)
                        v = cp(d2, n[:, :, 128:129], [k])
                        v = stt(dn[:, i:i + 2], dn[:, i:i + 2], -1.0, dn[:, i:i + 2], ALU.mult, ALU.max, [v])
                        v = tt(dn[:, i:i + 2], dn[:, i:i + 2], T["em_ap"][:, i:i + 2], ALU.max, [v, T["em"]])
                        v = recip(rec[:, i:i + 2], dn[:, i:i + 2], [v])
                        v = tt(headed(qk[:, t, h0 * P:(h0 + 2) * P], 2), n[:, :, 0:128],
                               rec[:, i:i + 2].unsqueeze(2).to_broadcast([P, 2, 128]), ALU.mult, [v, T["qk_read"]])
                        bank_free[b] = [v]
                        T["hA"].append(v)

            def recall_norm():
                ss = col(8)
                a = act(tmp, qk, ACT.Square, [T["hA"], T["kd"], T["sq2"]])
                v = red(ss, tmp.rearrange("p t (h e) -> p (t h) e", e=128), ALU.add, [a])
                rr, p = rstd(ss, 8, 128, [v])
                T["hA2"] = []
                for t in range(2):
                    h3 = headed(qk[:, t, :], 4)
                    v = tt(h3, h3, rr[:, 4 * t:4 * t + 4].unsqueeze(2).to_broadcast([P, 4, 128]), ALU.mult, [p])
                    v = tt(qk[:, t, :], qk[:, t, :], bcp1("oln"), ALU.mult, [v, t_bc])
                    v = tt(qk[:, t, :], qk[:, t, :], mo[:, t, :], ALU.mult, [v, T["sig_mo"]])
                    T["hA2"].append(v)

            def sigmoids(w):
                T[("sig", w)] = act(gab[:, w, :, :], gab[:, w, :, :], ACT.Sigmoid, [T[f"g{w}0"], T[f"g{w}1"]])

            def sigmoid_mo():
                T["sig_mo"] = act(mo, mo, ACT.Sigmoid, [T["mo"]])

            def part_turn(src, tok, c_at, key):
                for c0 in (0, 2):
                    b = chain_bank()
                    for c in (c0, c0 + 1):
                        for t in range(2):
                            k = tr(pb[b][:, (c - c0) * S + t * P:(c - c0) * S + (t + 1) * P],
                                   src[:, t, c * P:(c + 1) * P], [tok, bank_free[b]], inc=(c == c0 + 1 and t == 1))
                    hh = HTh[:, c_at + c0:c_at + c0 + 2, :].rearrange("p k t -> p (k t)")
                    hl = HTl[:, c_at + c0:c_at + c0 + 2, :].rearrange("p k t -> p (k t)")
                    th = act(hh, pb[b][:, :], ACT.Copy, [k, ht_free])
                    tl = tt(hl, pb[b][:, :], hh.bitcast(F32), ALU.subtract, [k, th, ht_free])
                    bank_free[b] = [tl]
                    T[(key, c0)] = [th, tl]

            g_small()
            if layer == 0:
                bias_table()
            gates_a()
            T["ones"] = PO.put(lambda e: e.memset(vx[:, :, :, 128:129], 1.0), [fr])
            g_copy(lambda t: qk[:, t, :], "qk")
            gates_b()
            qk_turn()
            g_query()
            gates_c()
            key_norm()
            g_copy(lambda t: vx[:, t, :, 0:128], "mv", form="p (h e) -> p h e")
            decay()
            sw_turn()
            scores()
            g_copy(lambda t: mo[:, t, :], "mo")
            logits(0)
            recall()
            g_copy(lambda t: gab[:, 0, t, 0:512], "g00")
            logits(1)
            soft(0)
            sigmoid_mo()
            recall_norm()
            g_copy(lambda t: gab[:, 0, t, 512:1024], "g01")
            p_turn(0)
            soft(1)
            part_turn(qk, T["hA2"], 0, "hAT")
            g_copy(lambda t: gab[:, 1, t, 0:512], "g10")
            attend(0)
            p_turn(1)
            g_copy(lambda t: gab[:, 1, t, 512:1024], "g11")
            attend(1)
            sigmoids(0)
            sigmoids(1)

            dA = product(HTh, HTl, [0, 1, 2, 3], lambda c, t: T[("hAT", c // 2 * 2)], 1024, 1, WIDE)
            for n in range(2):
                for t in range(2):
                    b = OB[t][n]
                    gs = gab[:, 0, t, n * 512:(n + 1) * 512]
                    v = tt(gs, gs, pb[b][:, :], ALU.mult, [dA[(t, n)], T[("sig", 0)]])
                    bank_free[b] = [v]
                    T[("a", t, n)] = v
            part_turn(sq, [T[("hB", 0)], T[("hB", 1)]], 4, "hBT")
            toks = {}

            def half(n, done):
                for t in range(2):
                    b = 4 + OB[t][n]
                    gs = gab[:, 1, t, n * 512:(n + 1) * 512]
                    v = tt(gs, gs, pb[b][:, :], ALU.mult, [done[t], T[("sig", 1)]])
                    bank_free[b] = [v]
                    T[("m", t, n)] = tt(gs, gs, gab[:, 0, t, n * 512:(n + 1) * 512], ALU.add, [v, T[("a", t, n)]])

            def mixed(lo, hi):
                for c in range(lo, hi):
                    turn_chunk(toks, c, lambda t: gab[:, 1, t, c * P:(c + 1) * P], lambda t: T[("m", t, c // 4)],
                               (4, 6, 4, 6, 5, 7, 5, 7)[c])()

            used = tail_product(HTh, HTl, [4, 5, 6, 7], lambda c, t: T[("hBT", (c - 4) // 2 * 2)], WIDE4, True, half,
                                lambda: mixed(0, 4))
            for i in range(HT_SLOTS):
                ht_free[i] = [used]
            state["later"] = lambda: mixed(4, 8)
            state["xt_free"] = [into_x(XTh, XTl, list(range(KD)), lambda c, t: toks[c], 1.0, following)]
            sh["s"] = [[T["hA2"]], [T["hA2"]]]
            sh["h"] = [[T[("hB", 1)]], [T[("hB", 1)]]]
            state["free1"] = [x_tok[(1, 1)], toks[KD - 1], T["hA2"]]

        def gated_input(layer, norm, following):
            dg = product(XTh, XTl, list(range(KD)), norm.ready, 1024, 1, WIDE)
            state["xt_free"] = [freed[at["use"] - 1]]
            tmp = part("gab", form="p (w t n) -> p w t n", w=2, t=2)
            sig = {}
            for n in range(2):
                for t in range(2):
                    b = OB[t][n]
                    sig[(t, n)] = act(tmp[:, 0, t, n * 512:(n + 1) * 512], pb[b][:, :], ACT.Sigmoid,
                                      [dg[(t, n)], norm.r_tok, state["free1"]], scale=norm.r[:, t:t + 1])
                    bank_free[b] = [sig[(t, n)]]
            lows = []

            def half(n, done):
                for t in range(2):
                    b = 4 + OB[t][n]
                    o = tmp[:, 0, t, n * 512:(n + 1) * 512]
                    v = tt(o, o, pb[b][:, :], ALU.mult, [sig[(t, n)], done[t]])
                    bank_free[b] = [v]
                    xs = X[:, t, n * 512:(n + 1) * 512]
                    x_tok[(t, n)] = [tt(xs, xs, o, ALU.add, [v, state["x_read"]])]
                for low in lows:
                    low()

            used = tail_product(PTh, PTl, [0, 1], lambda c, t: state["pT"], WIDE4, True, half,
                                lambda: lows.extend(following.chunks(0, 4)))
            state["later"] = following.rest
            state["free1"] = [x_tok[(1, 1)], used]

        def load_ple(layer):
            return load(PO, part("gab")[:, 2048:2560].rearrange("p (k t) -> p k t", k=2), d["pT"][layer],
                        state["free1"])

        def split_ple(t_p):
            pin = part("gab")[:, 2048:2560].rearrange("p (k t) -> p k t", k=2)
            th = act(PTh[:, :, :], pin, ACT.Copy, [t_p, state["free1"]])
            tl = tt(PTl[:, :, :], pin, PTh[:, :, :].bitcast(F32), ALU.subtract, [th])
            state["pT"] = [th, tl]

        norm = Norm(0, TO_FFN)
        for low in norm.chunks(0, 4):
            low()
        state["later"] = norm.rest
        for layer in range(2):
            new_layer()
            small_inputs1(layer)
            after = Norm(4 * layer + 1, TO_MIX)
            ffn(norm, after)
            norm, after = after, Norm(4 * layer + 2, TO_FFN)
            mixer1(layer, norm, after)
            norm, after = after, Norm(4 * layer + 3, TO_MIX)
            t_pin = load_ple(layer)
            ffn(norm, after, lambda: split_ple(t_pin))
            norm, after = after, Norm(4 * layer + 4, AFTER_GATE)
            gated_input(layer, norm, after)
            norm = after
        first.close()

        c2, n2 = spans([("Pg", 2048), ("slope", 2048), ("bc", 1280), ("wg", 256), ("cw", 64), ("z", 512), ("zp", 572),
                        ("acc", 512), ("y", 2048), ("q", 1024), ("k", 1024), ("v", 1024), ("qT", 1024), ("kT", 1024),
                        ("up", 512), ("dT", 1024), ("pr", 4096), ("aT", 2048), ("yc", 512)])
        scr2 = sb("scr2", [P, n2])
        fr1 = state["free1"]

        def part2(name, **kw):
            a = scr2[:, c2[name][0]:c2[name][1]]
            return a.rearrange(kw["form"], **{k: v for k, v in kw.items() if k != "form"}) if kw else a

        def bcp2(name):
            return part2("bc")[:, bc2[name][0]:bc2[name][1]]

        Pg = part2("Pg", form="p (g s t) -> p g s t", g=4, s=2)
        slope = part2("slope", form="p (h t k) -> p h t k", h=4, t=2)
        zp = part2("zp", form="p (c n) -> p c n", c=2)
        cw = part2("cw")
        wg = part2("wg", form="p (g n) -> p g n", g=4)
        state["free2"] = fr1

        def small_inputs2(layer):
            fr = state["free2"]
            state["t_bc2"] = load(PO, part2("bc"), d["bc2"][layer:layer + 1, :].to_broadcast([P, 1280]), fr)
            state["t_cw"] = load(PO, cw, d["cw"][layer], fr)
            state["t_wg"] = load(PO, wg[0:64, :, :], d["wg"][layer], fr)
            if layer == 0:
                state["t_slope"] = load(PO, slope, d["slope"], fr)
                state["t_pg"] = load(PO, Pg, d["Pg"], fr)
                state["z_pad"] = [PO.put(lambda e: e.memset(zp[:, :, 0:15], 0.0), [fr]),
                                  PO.put(lambda e: e.memset(zp[:, :, 271:286], 0.0), [fr])]
                state["post_gain"], state["post_tok"] = bcp2("post"), state["t_bc2"]
                state["pcol"] = tt(pcol[:, :], gcol[:, 14 * KD - KD * 3:14 * KD - KD * 2], postc[:, :], ALU.mult,
                                   [t_gcol, t_pcol])

        def mixer2(layer, norm, following):
            fr = state["free2"]
            lam0 = 0.8 - 0.6 * math.exp(-0.3 * layer)
            t_bc, t_cw, t_wg = state["t_bc2"], state["t_cw"], state["t_wg"]
            h0 = 4 + 9 * layer
            gq, gk, gs, gp0, gp1, lg0, lg1, lb0, lb1 = (hcol[:, h0 + i:h0 + i + 1] for i in range(9))
            z = part2("z", form="p (t n) -> p t n", t=2)
            acc = part2("acc", form="p (c t) -> p c t", c=2)
            yc = part2("yc", form="p (c t) -> p c t", c=2)
            y = part2("y", form="p (t n) -> p t n", t=2)
            q, k_, v_ = (part2(n, form="p (t n) -> p t n", t=2) for n in ("q", "k", "v"))
            qT, kT = (part2(n, form="p (c t) -> p c t", c=4) for n in ("qT", "kT"))
            up = part2("up", form="p (t n) -> p t n", t=2)
            dT = part2("dT", form="p (g t) -> p g t", g=4)
            pr = part2("pr", form="p (t m j) -> p t m j", t=2, m=8)
            aT = part2("aT", form="p (t n) -> p t n", t=2)
            tmp = sbuf_s[:, :, :, :].rearrange("p a b c -> p (a b c)").rearrange("p (t n) -> p t n", t=2)
            tmp2 = sbuf_h[:, :, :, :].rearrange("p a b c -> p (a b c)").rearrange("p (t n) -> p t n", t=2)
            T = {}
            toks = {}
            turn_bank = {"n": 0}
            pair = {"n": 0}

            def chain_bank():
                turn_bank["n"] += 1
                return 4 + (turn_bank["n"] - 1) % 4

            def group(ncols, kper=2):
                b0 = 2 * (pair["n"] % 2)
                pair["n"] += 1
                banks = [[(b0 + t, 0, ncols)] for t in range(2)]
                done = product(XTh, XTl, list(range(KD)), norm.ready, ncols, kper, banks)
                state["xt_free"] = [done[(1, 0)]]
                return b0, done

            def g_copy(dst_, key, ncols=512, kper=2):
                b0, done = group(ncols, kper)
                T[key] = []
                for t in range(2):
                    a = act(dst_[:, t, :], pb[b0 + t][:, 0:ncols], ACT.Copy, [done[(t, 0)], norm.r_tok, fr],
                            scale=norm.r[:, t:t + 1])
                    bank_free[b0 + t] = [a]
                    T[key].append(a)

            def lam():
                lr = bcp2("lam").rearrange("p (a b e) -> p a b e", a=2, b=2)
                pl = col(128).rearrange("p (a e) -> p a e", a=2)
                v = tt(pl, lr[:, :, 0, :], lr[:, :, 1, :], ALU.mult, [t_bc])
                s2 = col(2)
                v = red(s2, pl, ALU.add, [v])
                a = act(s2, s2, ACT.Exp, [v])
                nl = col(1)
                v = tt(nl, s2[:, 1:2], s2[:, 0:1], ALU.subtract, [a])
                T["nlam"] = ts(nl, nl, -lam0, None, ALU.add, after=[v])
                T["nlam_ap"] = nl

            def conv_in():
                b0, done = group(512)
                T["z"] = []
                for t in range(2):
                    b = pb[b0 + t]
                    a = act(tmp[:, t, 0:256], b[:, 256:512], ACT.Sigmoid, [done[(t, 0)], norm.r_tok, sh["s"]],
                            scale=norm.r[:, t:t + 1])
                    v = stt(z[:, t, :], b[:, 0:256], norm.r[:, t:t + 1], tmp[:, t, 0:256], ALU.mult, ALU.mult, [a, fr])
                    bank_free[b0 + t] = [v]
                    T["z"].append(v)

            def conv_turn():
                b = chain_bank()
                for c in range(2):
                    for t in range(2):
                        k = tr(pb[b][:, c * S + t * P:c * S + (t + 1) * P], z[:, t, c * P:(c + 1) * P],
                               [T["z"], bank_free[b]], inc=(c == 1 and t == 1))
                a = act(zp[:, :, 15:271], pb[b][:, :].rearrange("p (c t) -> p c t", c=2), ACT.Copy, [k, fr])
                bank_free[b] = [a]
                T["zp"] = [a, state["z_pad"]]
                T["z_read"] = k

            def conv_tap(j):
                for c in range(2):
                    src = zp[:, c, j:j + S]
                    w = cw[:, 31 * c + j:31 * c + j + 1]
                    if j == 0:
                        v = ts(acc[:, c, :], src, w, cw[:, 62 + c:63 + c], ALU.mult, ALU.add, [T["zp"], t_cw, fr])
                    else:
                        v = stt(acc[:, c, :], src, w, acc[:, c, :], ALU.mult, ALU.add, [T[("acc", c)]])
                    T[("acc", c)] = v

            def conv_back():
                b = chain_bank()
                for t in range(2):
                    for c in range(2):
                        k = tr(pb[b][:, t * S + c * P:t * S + (c + 1) * P], acc[:, c, t * P:(t + 1) * P],
                               [T[("acc", 0)], T[("acc", 1)], bank_free[b]], inc=(c == 1 and t == 1))
                mu, nmu, ss, sh_ = (col(2) for _ in range(4))
                for t in range(2):
                    a = act(z[:, t, :], pb[b][:, t * S:(t + 1) * S], ACT.Copy, [k, T["z_read"]], acc=mu[:, t:t + 1])
                bank_free[b] = [a]
                p = p_ts(nmu, mu, -1.0 / 256, 0.0, ALU.mult, ALU.add, [a])
                for t in range(2):
                    a = act(tmp[:, t, 0:256], z[:, t, :], ACT.Square, [p, a], bias=nmu[:, t:t + 1], acc=ss[:, t:t + 1])
                rr, p = rstd(ss, 2, 256, [a])
                p = PO.put(lambda e: e.tensor_tensor(sh_, nmu, rr, ALU.mult), [p])
                for t in range(2):
                    a = act(z[:, t, :], z[:, t, :], ACT.Identity, [p], scale=rr[:, t:t + 1], bias=sh_[:, t:t + 1])
                T["zn"] = a

            def conv_out():
                b = chain_bank()
                for c in range(2):
                    for t in range(2):
                        k = tr(pb[b][:, c * S + t * P:c * S + (t + 1) * P], z[:, t, c * P:(c + 1) * P],
                               [T["zn"], bank_free[b]], inc=(c == 1 and t == 1))
                for c, (g, bb) in enumerate(((lg0, lb0), (lg1, lb1))):
                    a = act(yc[:, c, :], pb[b][:, c * S:(c + 1) * S], ACT.Silu, [k, t_hcol, fr], scale=g, bias=bb)
                bank_free[b] = [a]
                th = act(XTh[:, 0:2, :], yc, ACT.Copy, [a, state["xt_free"]])
                tl = tt(XTl[:, 0:2, :], yc, XTh[:, 0:2, :].bitcast(F32), ALU.subtract, [th])
                toks[0] = toks[1] = [th, tl]

            def pool():
                T["dT"] = []
                for g0 in (0, 2):
                    b = chain_bank()
                    for g in (g0, g0 + 1):
                        for s in range(2):
                            k = mm(pb[b][0:64, (g - g0) * S:(g - g0 + 1) * S], up[:, s, g * 64:(g + 1) * 64],
                                   Pg[:, g, s, :], s == 0, s == 1, [T["up"], state["t_pg"], bank_free[b]],
                                   inc=(g == g0 + 1 and s == 1))
                    a = act(dT[0:64, g0:g0 + 2, :].rearrange("p g t -> p (g t)"), pb[b][0:64, :], ACT.Copy, [k, fr])
                    bank_free[b] = [a]
                    T["dT"].append(a)

            def pool_out():
                b = chain_bank()
                for t in range(2):
                    for g in range(4):
                        k = mm(pb[b][:, t * S + g * 64:t * S + (g + 1) * 64], dT[0:64, g, t * P:(t + 1) * P],
                               wg[0:64, g, :], True, True, [T["dT"], t_wg, bank_free[b]], inc=(t == 1 and g == 3))
                a = act(y[:, :, 256:512], pb[b][:, :].rearrange("p (t n) -> p t n", t=2), ACT.Copy, [k, fr])
                bank_free[b] = [a]
                T["y_pool"] = a

            def head_turn(src, key, dst_, gain):
                T[key + "T"] = []
                for c0 in (0, 2):
                    b = chain_bank()
                    for c in (c0, c0 + 1):
                        for t in range(2):
                            k = tr(pb[b][:, (c - c0) * S + t * P:(c - c0) * S + (t + 1) * P],
                                   src[:, t, c * P:(c + 1) * P], [T[key], bank_free[b]], inc=(c == c0 + 1 and t == 1))
                    a = act(dst_[:, c0:c0 + 2, :].rearrange("p c t -> p (c t)"), pb[b][:, :], ACT.Copy,
                            [k, fr, t_hcol], scale=gain)
                    bank_free[b] = [a]
                    T[key + "T"].append(a)

            def logits(t):
                m = col(8)
                T[("m", t)] = m
                T[("lg", t)] = []
                for h0 in (0, 2):
                    bs = [chain_bank(), chain_bank()]
                    ks = []
                    for h in (h0, h0 + 1):
                        for c in range(2):
                            rows = slice(64 * c, 64 * c + 64)
                            k = mm(pb[bs[c]][:, (h - h0) * S:(h - h0 + 1) * S], qT[rows, h, t * P:(t + 1) * P],
                                   kT[rows, h, :], True, True, [T["qT"], T["kT"], bank_free[bs[c]]],
                                   inc=(h == h0 + 1))
                            ks.append(k)
                    for c in range(2):
                        for h in (h0, h0 + 1):
                            i = 4 * c + h
                            src = pb[bs[c]][:, (h - h0) * S:(h - h0 + 1) * S]
                            v = VE.put(lambda e, i=i, h=h, src=src: e.tensor_tensor_reduce(
                                pr[:, t, i, :], src, slope[:, h, t, :], 1.0, NEG, ALU.add, ALU.max, m[:, i:i + 1]),
                                [ks[2 + c], state["t_slope"], fr])
                            T[("lg", t, i)] = v
                        bank_free[bs[c]] = [v]

            def soft(t):
                m, den, rec = T[("m", t)], col(8), col(8)
                n = ts(m, m, -1.0, None, ALU.mult, after=[T[("lg", t, i)] for i in range(8)])
                es = [act(pr[:, t, i, :], pr[:, t, i, :], ACT.Exp, [n], bias=m[:, i:i + 1], acc=den[:, i:i + 1])
                      for i in (0, 4, 1, 5, 2, 6, 3, 7)]
                v = recip(rec, den, [es[7]])
                v = ts(rec[:, 4:8], rec[:, 4:8], T["nlam_ap"], None, ALU.mult, after=[v, T["nlam"]])
                w = [ts(pr[:, t, h, :], pr[:, t, h, :], rec[:, h:h + 1], None, ALU.mult, after=[v]) for h in range(4)]
                for h in range(4):
                    T[("a", t, h)] = stt(pr[:, t, h, :], pr[:, t, 4 + h, :], rec[:, 4 + h:5 + h], pr[:, t, h, :],
                                         ALU.mult, ALU.add, [w[h]])

            def a_turn(t):
                T[("aT", t)] = []
                for h0 in (0, 2):
                    b = chain_bank()
                    for i, (h, s) in enumerate([(h, s) for h in (h0, h0 + 1) for s in range(2)]):
                        k = tr(pb[b][:, i * P:(i + 1) * P], pr[:, t, h, s * P:(s + 1) * P],
                               [T[("a", t, h)], bank_free[b]], inc=(i == 3))
                    a = act(aT[:, t, (h0 // 2) * 512:(h0 // 2 + 1) * 512], pb[b][:, :], ACT.Copy, [k, fr])
                    bank_free[b] = [a]
                    T[("aT", t)].append(a)

            def attend(t):
                b = chain_bank()
                for h in range(4):
                    for s in range(2):
                        k = mm(pb[b][:, h * P:(h + 1) * P], aT[:, t, (2 * h + s) * P:(2 * h + s + 1) * P],
                               v_[:, s, h * P:(h + 1) * P], s == 0, s == 1,
                               [T[("aT", t)][h // 2], T["v"], bank_free[b]], inc=(h == 3 and s == 1))
                ss = col(4)
                a = act(tmp2[:, t, :], pb[b][:, :], ACT.Square, [k, sh["h"]])
                v = red(ss, headed(tmp2[:, t, :], 4), ALU.add, [a])
                rr, p = rstd(ss, 4, 128, [v], 1.0 - lam0)
                o = headed(y[:, t, 512:1024], 4)
                v = tt(o, headed(pb[b][:, :], 4), rr.unsqueeze(2).to_broadcast([P, 4, 128]), ALU.mult, [p, a, fr])
                bank_free[b] = [v]
                T[("y_attn", t)] = v

            def y_turn(c):
                gain = (None, None, gp0, gp1, gs, gs, gs, gs)[c]
                turn_chunk(toks, c, lambda t: y[:, t, c * P:(c + 1) * P],
                           lambda t: T["y_pool"] if c < 4 else T[("y_attn", t)], chain_bank(), gain, t_hcol)()

            state["bg_n"] = 5
            conv_in()
            lam()
            def g_head(dst_, key, buf, extra, wait):
                b0, done = group(512)
                head_norm(b0, done, norm, dst_, buf, extra, [wait, fr], T, key)

            g_head(q, "q", tmp2, 0.125, sh["h"])
            conv_turn()
            state["bg"] = [lambda j=j: conv_tap(j) for j in range(31)]
            g_head(k_, "k", tmp2, 1.0, T["q"])
            head_turn(q, "q", qT, gq)
            g_copy(v_, "v")
            head_turn(k_, "k", kT, gk)
            logits(0)
            soft(0)
            g_copy(up, "up", 256, 4)
            logits(1)
            a_turn(0)
            pool()
            while state["bg"]:
                state["bg"].pop(0)()
            soft(1)
            attend(0)
            pool_out()
            conv_back()
            a_turn(1)
            conv_out()
            for c in (2, 3):
                y_turn(c)
            attend(1)
            for c in range(4, 8):
                y_turn(c)
            state["bg_n"] = 0
            state["xt_free"] = [into_x(XTh, XTl, list(range(KD)), lambda c, t: toks[c], 1.0, following)]
            last = [T[("y_attn", 0)], T[("y_attn", 1)], T["zn"], toks[7]]
            sh["s"] = [last, last]
            sh["h"] = [last, last]
            state["free2"] = [x_tok[(1, 1)], toks[KD - 1], last]

        def post():
            ss = col(2)
            a = square_sum(ss)
            rr, p = rstd(ss, 2, D, [a])
            for t in range(2):
                v = stt(X[:, t, :], X[:, t, :], rr[:, t:t + 1], bcp2("post"), ALU.mult, ALU.mult, [p, state["t_bc2"]])
                x_tok[(t, 0)] = x_tok[(t, 1)] = [v]

        t_pcol = load(PO, postc[:, :], d["postc"])
        for layer in range(2):
            new_layer()
            if layer == 0:
                small_inputs2(0)
            after = Norm(8 + 3 * layer + 1, TO_MIX)
            if layer == 0:
                ffn(norm, after)
            else:
                ffn(norm, after, lambda: small_inputs2(1))
            norm, after = after, Norm(8 + 3 * layer + 2, TO_FFN)
            mixer2(layer, norm, after)
            norm = after
            after = NormTwice(0, TO_FFN, pcol[:, :], state["pcol"]) if layer == 0 else None
            ffn(norm, after)
            norm = after
            if layer == 0:
                state["free2"] = [state["free2"], x_tok[(1, 1)]]
        post()
        s_out = sem("s_out")
        for t in range(2):
            SP.put(lambda e, t=t: e.dma_start(out[t * P:(t + 1) * P, :], X[:, t, :]), [x_tok[(t, 0)]],
                   signal=(s_out, 16))
        assert at["use"] == n_units

        block = ctx.enter_context(nc.Block())

        @block.tensor
        def _(eng):
            PE.run(eng)

        @block.vector
        def _(eng):
            VE.run(eng)

        @block.scalar
        def _(eng):
            SE.run(eng)

        @block.gpsimd
        def _(eng):
            PO.run(eng)

        @block.sync
        def _(eng):
            SP.run(eng)
            eng.wait_ge(s_out, 32)


def bucket(dist):
    half = 16
    dd = np.maximum(dist, 0)
    large = half + (np.log(np.maximum(dd, 1) / half) / np.log(128 / half) * half).astype(np.int32)
    return np.where(dd < half, dd, np.minimum(large, 31)).astype(np.int32)


def constants():
    f = np.float32
    i = np.arange(S)
    ident = np.eye(P, dtype=f)
    tri = (i[:, None] <= i[None, :]).astype(f).reshape(2, P, S).transpose(1, 0, 2)
    eye = np.eye(S, dtype=f).reshape(2, P, S).transpose(1, 0, 2)
    cmask = np.zeros((P, S), f)
    cmask[:, :P] = np.where(np.arange(P)[:, None] <= np.arange(P)[None, :], 0.0, -NEG)
    sel = np.zeros((4, 4, P), f)
    for h in range(4):
        sel[h, h, :] = 1.0
    n = np.arange(384)
    dist = P - np.where(n < 256, n, n - 384)
    ok = (dist >= 0) & (dist < P)
    onehot = np.zeros((33, 384), f)
    onehot[bucket(dist), n] = 1.0
    onehot[:, ~ok] = 0.0
    onehot[32] = np.where(ok, 0.0, NEG)
    Pg = np.zeros((4, S, S), f)
    for g, w in enumerate((2, 4, 8, 16)):
        for t in range(S):
            lo, hi = max(t - w // 2, 0), min(t + w // 2, S)
            Pg[g, lo:hi, t] = f(1.0) / f(hi - lo)
            Pg[g, t, t] -= f(1.0)
    Pg = Pg.reshape(4, 2, P, S).transpose(2, 0, 1, 3)
    dd = np.abs(i[:, None] - i[None, :]).astype(f).reshape(2, P, S).transpose(1, 0, 2)
    slope = np.stack([-dd * f(2.0 ** (-8.0 * (h + 1) / 4)) for h in range(4)], 1)
    return {k: np.ascontiguousarray(v, dtype=f) for k, v in
            dict(ident=ident, tri=tri, eye=eye, cmask=cmask, sel=sel, onehot=onehot, Pg=Pg, slope=slope).items()}


def layout(a):
    units = []

    def rows(w, c0, c1, k0, n):
        return w[k0 * P:(k0 + n) * P, c0:c1].reshape(n, P, c1 - c0).transpose(1, 0, 2)

    def group(w, kper):
        for k0 in range(0, w.shape[0] // P, kper):
            units.append(rows(w, 0, w.shape[1], k0, kper).reshape(P, -1))

    def ffn(wg, wu, wo):
        for kind, g in ffn_order():
            if kind == "gu":
                for k0 in range(0, KD, 2):
                    u = np.stack([rows(wg, 256 * g, 256 * g + 256, k0, 2), rows(wu, 256 * g, 256 * g + 256, k0, 2)], 2)
                    units.append(u.reshape(P, -1))
            else:
                group(wo[256 * g:256 * g + 256], 1)

    for i in range(2):
        wi = a["ffn1_wi"][i]
        ffn(wi[:, :FF], wi[:, FF:], a["ffn1_wo"][i])
        w = a["w_in"][i]
        mq, mk, mv, mo, gi, sq, skv, ga, gb = np.split(w, [256, 512, 1024, 1536, 1544, 2056, 2312, 3336], axis=1)
        group(np.concatenate([gi, skv], 1), 2)
        group(np.concatenate([mq, mk], 1), 2)
        group(sq, 2)
        group(mv, 2)
        group(mo, 2)
        for x in (ga, gb):
            group(x[:, :512], 2)
            group(x[:, 512:], 2)
        group(a["w_a"][i], 1)
        group(a["w_b"][i], 1)
        group(a["w_out"][i], 1)
        wi = a["ffn2_wi"][i]
        ffn(wi[:, :FF], wi[:, FF:], a["ffn2_wo"][i])
        group(a["w_ple_gate"][i], 1)
        group(a["w_ple"][i], 1)
    for i in range(2):
        ffn(a["ffn1_w_gate_2"][i], a["ffn1_w_up_2"][i], a["ffn1_w_down_2"][i])
        conv, pool, q, k, v = np.split(a["w_in_2"][i], [512, 768, 1280, 1792], axis=1)
        group(conv, 2)
        group(q, 2)
        group(k, 2)
        group(v, 2)
        group(pool, 4)
        group(a["w_out_2"][i], 1)
        ffn(a["ffn2_w_gate_2"][i], a["ffn2_w_up_2"][i], a["ffn2_w_down_2"][i])
    cols = [u.shape[1] for u in units]
    W = np.zeros((len(units), P, UC), np.float32)
    for n, u in enumerate(units):
        W[n, :, :cols[n]] = u
    return W, cols


def kernel(**inputs):
    import concourse.bacc as bacc
    from concourse.bass_utils import run_bass_kernel_spmd as run

    a = {k: np.asarray(v) for k, v in inputs.items()}
    heads = [0, 2, 4, 6, 1, 3, 5, 7]

    def columns(v):
        return v.reshape(KD, P).T

    W, cols = layout(a)
    gains = []
    for i in range(2):
        gains += [a[n][i] for n in ("ffn1_norm", "mix_norm", "ffn2_norm", "ple_norm")]
    for i in range(2):
        gains += [a[n][i] for n in ("ffn1_norm_2", "mix_norm_2", "ffn2_norm_2")]
    bc1 = np.stack([np.concatenate([a["ml_out_norm"][i].reshape(-1), a["sinks"][i][heads], a["b_igate"][i],
                                    a["b_fgate"][i]]) for i in range(2)])
    bc2 = np.stack([np.concatenate([a["post_norm_2"][i], a["lambda_q1_2"][i], a["lambda_k1_2"][i],
                                    a["lambda_q2_2"][i], a["lambda_k2_2"][i]]) for i in range(2)])
    hcol = []
    for i in range(2):
        hcol += [np.tile(a["q_norm"][i], 2), np.tile(a["k_norm"][i], 2)]
    for i in range(2):
        hcol += [np.tile(a["q_norm_2"][i], 2), np.tile(a["k_norm_2"][i], 2), a["attn_subln_2"][i]]
        hcol += list(a["pool_scale_2"][i].reshape(2, P)) + list(a["conv_ln_gain_2"][i].reshape(2, P))
        hcol += list(a["conv_ln_bias_2"][i].reshape(2, P))
    cw = np.stack([np.concatenate([a["conv_dw_2"][i].reshape(31, 2, P).transpose(2, 1, 0).reshape(P, 62),
                                   a["conv_dw_bias_2"][i].reshape(2, P).T], 1) for i in range(2)])
    arrays = dict(constants())
    arrays.update(
        W=W,
        x=a["x"][0].reshape(2, P, D).transpose(1, 0, 2),
        gcol=np.concatenate([columns(g) for g in gains], 1),
        bc1=bc1, bc2=bc2, cw=cw, hcol=np.stack(hcol, 1), postc=columns(a["post_norm_2"][0]),
        rb=np.repeat(a["rel_bias"][:, heads], P, axis=1).reshape(32, 8, P),
        pT=np.stack([a["p"][i, 0].T.reshape(2, P, S).transpose(1, 0, 2) for i in range(2)]),
        wg=a["pool_w_2"].transpose(0, 2, 1, 3),
    )
    arrays = {k: np.ascontiguousarray(v) for k, v in arrays.items()}
    nc = bacc.Bacc("TRN2", target_bir_lowering=False, num_devices=1)
    d = {k: nc.dram_tensor("in_" + k, v.shape, F32, kind="ExternalInput").ap() for k, v in arrays.items()}
    d["scratch"] = nc.dram_tensor("scratch", (8, P, 384), F32, kind="Internal").ap()
    d["cols"] = cols
    out = nc.dram_tensor("out_0", (S, D), F32, kind="ExternalOutput").ap()
    program(nc, d, out)
    r = run(nc, [{"in_" + k: v for k, v in arrays.items()}], core_ids=[0])
    return np.asarray(r.results[0]["out_0"]).reshape(1, S, D)
```

```python
import math
from contextlib import ExitStack

import numpy as np
import concourse.bass as bass
from concourse import mybir

F32 = mybir.dt.float32
F32R = mybir.dt.float32r
BF16 = mybir.dt.bfloat16
ALU = mybir.AluOpType
ACT = mybir.ActivationFunctionType
AXX = mybir.AxisListType.X

P = 128
D = 1024
S = 256
KD = D // P
FF = 2816
NG = FF // 256
EPS = 1e-6
UC = 1024
NEG = -1.0e30
RAW_SLOTS = 4
W_SLOTS = 5
HT_SLOTS = 4
OUT2 = [2, 3, 4, 5, 6, 7, 0, 1]

BC1 = [("oln", 512), ("sink", 8), ("gb", 8)]
BC2 = [("post", 1024), ("lam", 256)]


def spans(items):
    out, at = {}, 0
    for name, n in items:
        out[name] = (at, at + n)
        at += n
    return out, at


def ffn_order():
    order = [("gu", 0)]
    for g in range(1, NG):
        order += [("gu", g), ("o", g - 1)]
    return order + [("o", NG - 1)]


class Line:

    def __init__(self, sem, serial=False):
        self.sem, self.n, self.prog, self.passed, self.serial = sem, 0, [], {}, serial

    def put(self, call, after=(), inc=True, signal=None):
        need = {}
        if self.serial and self.n:
            after = [after, (self.sem, self.n)]
        for sem, value in flat(after):
            if self.passed.get(sem.name, 0) < value:
                self.passed[sem.name] = value
                need[sem.name] = (sem, value)
        if signal is None and inc:
            self.n += 1
            signal = (self.sem, 1)
        self.prog.append((list(need.values()), call, signal))
        return (self.sem, self.n)

    def run(self, eng):
        for waits, call, signal in self.prog:
            for sem, value in waits:
                eng.wait_ge(sem, value)
            ins = call(eng)
            if signal is not None:
                ins.then_inc(signal[0], signal[1])


def flat(after):
    for x in after:
        if not x:
            continue
        if isinstance(x, tuple):
            yield x
        else:
            yield from flat(x)


def program(nc, d, out):
    ctx = ExitStack()
    with ctx:
        def sb(name, shape, dt=F32):
            return ctx.enter_context(nc.sbuf_tensor(name, shape, dt))

        def sem(name):
            return ctx.enter_context(nc.semaphore(name))

        PE, VE, SE, SP = (Line(sem("s_" + n)) for n in ("pe", "dve", "act", "sp"))
        PO = Line(sem("s_pool"), serial=True)

        raw = [sb(f"raw{i}", [P, UC]) for i in range(RAW_SLOTS)]
        whi = [sb(f"whi{i}", [P, UC], F32R) for i in range(W_SLOTS)]
        wlo = [sb(f"wlo{i}", [P, UC], F32R) for i in range(W_SLOTS)]
        HTh = sb("HTh", [P, 2 * HT_SLOTS, S], F32R)
        HTl = sb("HTl", [P, 2 * HT_SLOTS, S], F32R)
        XTh = sb("XTh", [P, KD, S], F32R)
        XTl = sb("XTl", [P, KD, S], F32R)
        X = sb("X", [P, 2, D])
        junk = sb("junk", [P, D], BF16)
        sbuf_s = sb("sbuf_s", [P, 2, 2, 256])
        sbuf_h = sb("sbuf_h", [P, 2, 2, 256])
        ident = sb("ident", [P, P])
        st = sb("st", [P, 2, 400])
        cst = sb("cst", [P, 4])
        gcol = sb("gcol", [P, 14 * KD])
        hcol = sb("hcol", [P, 22])
        pcol = sb("pcol", [P, KD])
        postc = sb("postc", [P, KD])
        pb = [ctx.enter_context(nc.psum_tensor(f"pb{i}", [P, 512], F32)) for i in range(8)]

        bank_free = [[] for _ in range(8)]

        def mm(o, l, r, start, stop, after=(), inc=False):
            return PE.put(lambda e: e.matmul(o, l, r, start=start, stop=stop), after, inc)

        def tr(o, i, after=(), inc=False):
            n = i.shape[0]
            return PE.put(lambda e: e.transpose(o, i, ident[0:n, 0:n]), after, inc)

        def act(o, i, f, after=(), scale=1.0, bias=None, acc=None):
            kw = {"scale": scale}
            if bias is not None:
                kw["bias"] = bias
            if acc is not None:
                kw["accum_out"] = acc
            return SE.put(lambda e: e.activation(o, i, f, **kw), after)

        def tt(o, a, b, op, after=()):
            return VE.put(lambda e: e.tensor_tensor(o, a, b, op), after)

        def stt(o, a, s, b, op0, op1, after=()):
            return VE.put(lambda e: e.scalar_tensor_tensor(out=o, in0=a, scalar=s, in1=b, op0=op0, op1=op1), after)

        def ts(o, a, s1, s2, op0, op1=None, after=()):
            if op1 is None:
                return VE.put(lambda e: e.tensor_scalar(o, a, s1, None, op0), after)
            return VE.put(lambda e: e.tensor_scalar(o, a, s1, s2, op0, op1), after)

        def cp(o, i, after=()):
            return VE.put(lambda e: e.tensor_copy(o, i), after)

        def red(o, i, op, after=()):
            return VE.put(lambda e: e.tensor_reduce(o, i, AXX, op), after)

        def recip(o, i, after=()):
            return VE.put(lambda e: e.reciprocal(o, i), after)

        def p_pow(o, a, b, after=()):
            return PO.put(lambda e: e.tensor_tensor(o, a, b, ALU.pow), after)

        def load(line, dst, src, after=()):
            s = sem(f"s_ld{len(loads)}")
            loads.append(s)
            line.put(lambda e: e.dma_start(dst, src), after, signal=(s, 16))
            return (s, 16)

        loads = []

        units = d["cols"]
        n_units = len(units)
        raw_sem = [sem(f"s_raw{i}") for i in range(RAW_SLOTS)]
        dma_tok, split_tok, freed = {}, {}, {}
        at = {"dma": 0, "split": 0, "use": 0}

        def stream_dma(to):
            while at["dma"] < min(to, n_units) and at["dma"] - RAW_SLOTS < at["split"]:
                u = at["dma"]
                c = units[u]
                dst, src = raw[u % RAW_SLOTS][:, 0:c], d["W"][u, :, 0:c]
                after = split_tok[u - RAW_SLOTS] if u >= RAW_SLOTS else ()
                SP.put(lambda e, dst=dst, src=src: e.dma_start(dst, src), after,
                       signal=(raw_sem[u % RAW_SLOTS], 16))
                dma_tok[u] = (raw_sem[u % RAW_SLOTS], 16 * (u // RAW_SLOTS + 1))
                at["dma"] += 1

        def stream_split(to):
            while at["split"] < min(to, n_units):
                u = at["split"]
                if u >= W_SLOTS and u - W_SLOTS not in freed:
                    return
                stream_dma(u + 1)
                c = units[u]
                r, h, l = raw[u % RAW_SLOTS][:, 0:c], whi[u % W_SLOTS][:, 0:c], wlo[u % W_SLOTS][:, 0:c]
                slot = freed.get(u - W_SLOTS)
                th = act(h, r, ACT.Copy, [dma_tok[u], slot])
                tl = tt(l, r, h.bitcast(F32), ALU.subtract, [dma_tok[u], slot, th])
                split_tok[u] = [th, tl]
                at["split"] += 1
                stream_dma(u + 1 + RAW_SLOTS)

        def next_unit():
            u = at["use"]
            at["use"] += 1
            stream_split(u + W_SLOTS - 1)
            assert at["split"] > u
            return u, whi[u % W_SLOTS], wlo[u % W_SLOTS], split_tok[u]

        chains = []
        side_banks = [4, 5, 6, 7]

        def advance():
            for g in list(chains):
                if next(g, chains) is chains:
                    chains.remove(g)

        def drain():
            while chains:
                advance()

        def need(T, key):
            while key not in T:
                assert chains, key
                advance()
            return T[key]

        def have(T, *keys):
            while any(k not in T for k in keys):
                yield

        def pause(n):
            for _ in range(n):
                yield

        def grab(n):
            while len(side_banks) < n:
                yield
            return [side_banks.pop(0) for _ in range(n)]

        def give(b, tok):
            bank_free[b] = [tok]
            side_banks.append(b)

        def product(lh, ll, chunks, ready, ncols, kper, banks, begin=True, end=True, hook=None):
            done = {}
            nk = len(chunks)
            for k0 in range(0, nk, kper):
                advance()
                u, h, l, got = next_unit()
                jobs = [(t, b) for b in range(len(banks[0])) for t in range(2)]
                for j, (t, b) in enumerate(jobs):
                    if 2 * j == len(jobs) and state["halves"]:
                        advance()
                    if hook is not None and hook[:2] == (k0 // kper, j):
                        hook[2]()
                    bank, c0, n = banks[t][b]
                    for k in range(k0, k0 + kper):
                        c = chunks[k]
                        wc = (k - k0) * ncols + c0
                        o = pb[bank][:, 0:n]
                        ah, al = lh[:, c, t * P:(t + 1) * P], ll[:, c, t * P:(t + 1) * P]
                        bh, bl = h[:, wc:wc + n], l[:, wc:wc + n]
                        first, last = begin and k == 0, end and k == nk - 1
                        mm(o, ah, bh, first, False, [got, ready(c, t), bank_free[bank] if first else ()])
                        mm(o, ah, bl, False, False)
                        fin = j == len(jobs) - 1 and k == k0 + kper - 1
                        tok = mm(o, al, bh, False, last, inc=last or fin)
                        if last:
                            done[(t, b)] = tok
                        if fin:
                            freed[u] = tok
                if k0 + kper >= 2:
                    run_later()
            return done

        small = {"set": 0, "at": 0}

        def col(n):
            a = st[:, small["set"], small["at"]:small["at"] + n]
            small["at"] += n
            assert small["at"] <= 400
            return a

        def new_layer():
            small["set"] ^= 1
            small["at"] = 0

        def rstd(ss, n, count, after, extra=1.0):
            v, r = col(n), col(n)
            a = ts(v, ss, 1.0 / (count * extra * extra), EPS / (extra * extra), ALU.mult, ALU.add, after)
            a = p_pow(r, v, cst[:, 0:1].to_broadcast([P, n]), [a, t_cst])
            return r, a

        t_id = load(SP, ident[:, :], d["ident"])
        t_xs = [load(SE, X[:, :, n * 512:(n + 1) * 512], d["x"][:, :, n * 512:(n + 1) * 512]) for n in range(2)]
        t_gcol = load(PO, gcol[:, :], d["gcol"])
        t_hcol = load(PO, hcol[:, :], d["hcol"])
        t_cst = PO.put(lambda e: e.memset(cst[:, :], -0.5))
        x_tok = {(t, n): [t_xs[n]] for t in range(2) for n in range(2)}
        state = {"xt_free": [], "junk": [], "later": None, "halves": False}

        def run_later():
            if state["later"] is not None:
                call, state["later"] = state["later"], None
                call()

        ht_free = [[] for _ in range(HT_SLOTS)]
        OB = [[0, 1], [2, 3]]
        WIDE = [[(OB[t][n], n * 512, 512) for n in range(2)] for t in range(2)]
        WIDE4 = [[(4 + OB[t][n], n * 512, 512) for n in range(2)] for t in range(2)]

        def turn_chunk(toks, c, src, tok, bank, gain=None, gain_tok=None, dh=None, dl=None, free=None):
            if dh is None:
                dh, dl, free = XTh, XTl, state["xt_free"]
            for t in range(2):
                k = tr(pb[bank][:, t * P:(t + 1) * P], src(t), [tok(t), bank_free[bank], t_id], inc=(t == 1))
            o = pb[bank][:, 0:S]
            th = act(dh[:, c, :], o, ACT.Copy, [k, free, gain_tok], scale=1.0 if gain is None else gain)

            def low():
                hi = dh[:, c, :].bitcast(F32)
                if gain is None:
                    tl = tt(dl[:, c, :], o, hi, ALU.subtract, [k, th])
                else:
                    tl = stt(dl[:, c, :], o, gain, hi, ALU.mult, ALU.subtract, [k, th])
                bank_free[bank] = [tl]
                toks[c] = [th, tl]
                state["xt_read"] = k
            return low

        def square_sum(ss):
            for t in range(2):
                a = act(junk[:, :], X[:, t, :], ACT.Square, [x_tok[(t, 0)], x_tok[(t, 1)], state["junk"]],
                        acc=ss[:, t:t + 1])
                state["junk"] = [a]
            return a

        TO_FFN = [4, 5, 6, 7, 6, 7, 0, 2]
        TO_MIX = [4, 5, 6, 7, 4, 5, 6, 7]
        AFTER_GATE = [0, 2, 4, 5, 1, 3, 6, 7]

        class Norm:

            def __init__(self, which, banks, gains=None, gains_tok=None):
                self.toks, self.r, self.r_tok, self.banks = {}, None, None, banks
                self.gains = gcol[:, which * KD:(which + 1) * KD] if gains is None else gains
                self.gains_tok = t_gcol if gains is None else gains_tok

            def ready(self, c, t):
                return self.toks[c]

            def chunks(self, lo, hi):
                return [self.chunk(c) for c in range(lo, hi)]

            def chunk(self, c):
                return turn_chunk(self.toks, c, lambda t: X[:, t, c * P:(c + 1) * P], lambda t: x_tok[(t, c // 4)],
                                  self.banks[c], self.gains[:, c:c + 1], self.gains_tok)

            def rest(self):
                for c in range(4, 8):
                    self.chunks(c, c + 1)[0]()
                ss = col(2)
                a = square_sum(ss)
                self.r, self.r_tok = rstd(ss, 2, D, [a])
                state["x_read"] = [a, state["xt_read"]]

        class NormInHT(Norm):
            PLACE = [0, 1, 6, 7, 2, 3, 4, 5]

            def chunk(self, c):
                at_ = self.PLACE[c]
                return turn_chunk(self.toks, at_, lambda t: X[:, t, c * P:(c + 1) * P], lambda t: x_tok[(t, c // 4)],
                                  self.banks[c], self.gains[:, c:c + 1], self.gains_tok, HTh, HTl, ht_free[at_ // 2])

        class NormTwice(Norm):

            def rest(self):
                for c in range(4, 8):
                    self.chunks(c, c + 1)[0]()
                turned = state["xt_read"]
                s1, s2, both = col(2), col(2), col(2)
                a = square_sum(s1)
                r1, p1 = rstd(s1, 2, D, [a])
                for t in range(2):
                    v = stt(X[:, t, :], X[:, t, :], r1[:, t:t + 1], state["post_gain"], ALU.mult, ALU.mult,
                            [p1, turned, state["post_tok"]])
                    x_tok[(t, 0)] = x_tok[(t, 1)] = [v]
                a = square_sum(s2)
                r2, p2 = rstd(s2, 2, D, [a])
                self.r, self.r_tok = both, PO.put(lambda e: e.tensor_tensor(both, r1, r2, ALU.mult), [p1, p2])
                state["x_read"] = [a, turned]

        def tail_product(lh, ll, chunks, ready, banks, begin, half, between):
            if len(chunks) > 2:
                product(lh, ll, chunks[:-2], ready, 1024, 1, banks, begin=begin, end=False)
                begin = False
                if lh is XTh:
                    state["xt_free"] = [freed[at["use"] - 1]]
            drain()
            two = [next_unit(), next_unit()]
            for n in range(2):
                done = {}
                for t in range(2):
                    bank, c0, w = banks[t][n]
                    o = pb[bank][:, 0:w]
                    if n == 1 and t == 1:
                        between()
                    for i, (c, (u, h, l, got)) in enumerate(zip(chunks[-2:], two)):
                        ah, al = lh[:, c, t * P:(t + 1) * P], ll[:, c, t * P:(t + 1) * P]
                        first = begin and i == 0
                        mm(o, ah, h[:, c0:c0 + w], first, False, [got, ready(c, t), bank_free[bank] if first else ()])
                        mm(o, ah, l[:, c0:c0 + w], False, False)
                        tok = mm(o, al, h[:, c0:c0 + w], False, i == 1, inc=(i == 1))
                    done[t] = tok
                half(n, done)
            for u, _, _, _ in two:
                freed[u] = tok
            return tok

        def into_x(lh, ll, chunks, ready, factor, norm, begin=True):
            lows = []

            def half(n, done):
                for t in range(2):
                    xs = X[:, t, n * 512:(n + 1) * 512]
                    b = OB[t][n]
                    tok = stt(xs, pb[b][:, :], factor, xs, ALU.mult, ALU.add, [done[t], state["x_read"]])
                    bank_free[b] = [tok]
                    x_tok[(t, n)] = [tok]
                    if n == 1:
                        for low in lows[2 * t:2 * t + 2]:
                            low()

            def between():
                if norm is not None:
                    lows.extend(norm.chunks(0, 4))
                    for _ in range(2):
                        lows.pop(0)()
                    lows[:0] = [lambda: None] * 2

            tok = tail_product(lh, ll, chunks, ready, WIDE, begin, half, between)
            if norm is not None:
                state["later"] = norm.rest
            return tok

        ht_tok = {}
        sh = {"s": [[], []], "h": [[], []]}

        def ffn(norm, following, mid=None):
            h_tok = {}

            def gate_up(g):
                q = g % 2
                b0 = 4 + 2 * q
                banks = [[(b0 + t, 0, 512)] for t in range(2)]
                done = product_gu(g, banks)
                toks = []
                for t in range(2):
                    b = pb[b0 + t]
                    a = act(sbuf_s[:, q, t, :], b[:, 0:256], ACT.Silu, [done[t], norm.r_tok, sh["s"][q]],
                            scale=norm.r[:, t:t + 1])
                    v = stt(sbuf_h[:, q, t, :], b[:, 256:512], norm.r[:, t:t + 1], sbuf_s[:, q, t, :],
                            ALU.mult, ALU.mult, [a, sh["h"][q]])
                    bank_free[b0 + t] = [v]
                    toks.append(v)
                sh["s"][q] = toks
                h_tok[g] = toks

            def product_gu(g, banks):
                done = {}
                for i in range(4):
                    if i == 2 and g >= 1:
                        turn(g - 1)
                    u, h, l, got = next_unit()
                    for t in range(2):
                        if (i, t) == (1, 0):
                            run_later()
                        bank = banks[t][0][0]
                        o = pb[bank][:, :]
                        for k in (2 * i, 2 * i + 1):
                            ah, al = XTh[:, k, t * P:(t + 1) * P], XTl[:, k, t * P:(t + 1) * P]
                            w0 = (k % 2) * 512
                            mm(o, ah, h[:, w0:w0 + 512], k == 0, False,
                               [got, norm.ready(k, t), bank_free[bank] if k == 0 else ()])
                            mm(o, ah, l[:, w0:w0 + 512], False, False)
                            last = k == KD - 1
                            fin = t == 1 and k % 2 == 1
                            tok = mm(o, al, h[:, w0:w0 + 512], False, last, inc=last or fin)
                            if last:
                                done[t] = tok
                            if fin:
                                freed[u] = tok
                                state["xt_free"] = [tok]
                return done

            def turn(g):
                q, slot = g % 2, g % HT_SLOTS
                bank = 4 + 2 * q
                for k in range(2):
                    for t in range(2):
                        p = tr(pb[bank][:, k * S + t * P:k * S + (t + 1) * P], sbuf_h[:, q, t, k * P:(k + 1) * P],
                               [h_tok[g], bank_free[bank]], inc=(k == 1 and t == 1))
                sh["h"][q] = [p]
                hh = HTh[:, 2 * slot:2 * slot + 2, :].rearrange("p k t -> p (k t)")
                hl = HTl[:, 2 * slot:2 * slot + 2, :].rearrange("p k t -> p (k t)")
                th = act(hh, pb[bank][:, :], ACT.Copy, [p, ht_free[slot]])
                tl = tt(hl, pb[bank][:, :], hh.bitcast(F32), ALU.subtract, [p, th, ht_free[slot]])
                bank_free[bank] = [tl]
                ht_tok[slot] = [th, tl]

            def down(g):
                slot = g % HT_SLOTS
                chunks = [2 * slot, 2 * slot + 1]
                if g == NG - 1:
                    into_x(HTh, HTl, chunks, lambda c, t: ht_tok[slot], 0.5, following, begin=False)
                else:
                    product(HTh, HTl, chunks, lambda c, t: ht_tok[slot], 1024, 1, WIDE, begin=(g == 0), end=False,
                            hook=(1, 0, lambda: turn(NG - 1)) if g == NG - 2 else None)
                ht_free[slot] = [freed[at["use"] - 1]]

            for kind, g in ffn_order():
                if kind == "gu":
                    gate_up(g)
                    if g == 2 and mid is not None:
                        mid()
                else:
                    down(g)

        c1, n1 = spans([("tri", 512), ("eye", 512), ("cmask", 256), ("sel", 512), ("bc", 528), ("bias", 2048),
                        ("sq", 1024), ("sqT", 1024), ("kT", 512), ("qk", 1024), ("qkT", 1024),
                        ("vx", 1032), ("E", 1536), ("pr", 3072), ("prT", 3072), ("mo", 1024), ("gab", 4096),
                        ("rows", 512)])
        bc1, _ = spans(BC1)
        bc2, _ = spans(BC2)
        first = ExitStack()
        scr = first.enter_context(nc.sbuf_tensor("scr1", [P, n1], F32))
        PTh = first.enter_context(nc.sbuf_tensor("PTh", [P, 2, S], F32R))
        PTl = first.enter_context(nc.sbuf_tensor("PTl", [P, 2, S], F32R))

        def part(name, **kw):
            a = scr[:, c1[name][0]:c1[name][1]]
            return a.rearrange(kw["form"], **{k: v for k, v in kw.items() if k != "form"}) if kw else a

        tri = part("tri", form="p (s t) -> p s t", s=2)
        eye = part("eye", form="p (s t) -> p s t", s=2)
        cmask = part("cmask")
        sel = part("sel", form="p (h m) -> p h m", h=4)
        bias = part("bias", form="p (h j) -> p h j", h=8)

        def bcp1(name):
            return part("bc")[:, bc1[name][0]:bc1[name][1]]

        t_tri = load(PO, tri, d["tri"])
        t_eye = load(PO, eye, d["eye"])
        t_cm = load(PO, cmask, d["cmask"])
        t_sel = load(PO, sel[0:4, :, :], d["sel"])

        stage = part("pr", form="p (h n) -> p h n", h=8)
        rbT = part("prT")[:, 0:1024].rearrange("p (h m) -> p h m", h=8)
        oh = part("prT")[:, 1024:1408]
        t_rb1 = PO.put(lambda e: e.memset(rbT[32:33, :, :], 1.0))
        t_rb = load(PO, rbT[0:32, :, :], d["rb"])
        t_oh = load(PO, oh[0:33, :], d["onehot"])
        s_bo = sem("s_bo")
        skew = bass.AP(d["scratch"].tensor, 0, [[383, P], [384 * P, 8], [1, 256]])

        def bias_table():
            for h0 in range(0, 8, 2):
                bs = yield from grab(2)
                ks = []
                for b, h in zip(bs, (h0, h0 + 1)):
                    k = mm(pb[b][:, 0:384], rbT[0:33, h, :], oh[0:33, :], True, True,
                           [t_rb1, t_rb, t_oh, bank_free[b]], inc=True)
                    ks.append(k)
                yield
                for b, h, k in zip(bs, (h0, h0 + 1), ks):
                    v = cp(stage[:, h, :], pb[b][:, 0:384], [k])
                    give(b, v)
            PO.put(lambda e: e.dma_start(d["scratch"].rearrange("h p n -> p h n"), stage), [v], signal=(s_bo, 16))
            state["t_bias"] = load(PO, bias, skew, [(s_bo, 16)])
            state["pr_free"] = [(s_bo, 16), v]

        state["pr_free"] = []
        state["free1"] = []

        def small_inputs1(layer):
            state["t_bc1"] = load(PO, part("bc"), d["bc1"][layer:layer + 1, :].to_broadcast([P, 528]), state["free1"])

        def headed(a, n):
            return a.rearrange("p (h e) -> p h e", h=n)

        held = set()

        def head_norm(b0, done, norm, dst, buf, extra, wait, T, key):
            held.add(b0)
            for t in range(2):
                a = act(buf[:, t, :], pb[b0 + t][:, :], ACT.Square, [done[(t, 0)], norm.r_tok, wait],
                        scale=norm.r[:, t:t + 1])
            T[key + "_sq"] = a
            yield
            ss = col(16)
            v = red(ss, buf.rearrange("p t (h e) -> p (t h) e", e=64), ALU.add, [a])
            rr, p = rstd(ss, 16, 64, [v], extra)
            yield from pause(4 if state["halves"] else 1)
            toks = []
            for t in range(2):
                w = VE.put(lambda e, t=t: e.scalar_tensor_tensor(
                    out=headed(dst[:, t, :], 8), in0=headed(pb[b0 + t][:, :], 8), scalar=norm.r[:, t:t + 1],
                    in1=rr[:, 8 * t:8 * t + 8].unsqueeze(2).to_broadcast([P, 8, 64]), op0=ALU.mult, op1=ALU.mult),
                    [p, a, wait])
                bank_free[b0 + t] = [w]
                toks.append(w)
            T[key] = toks
            held.discard(b0)

        def turn_two(src, dst, key, T, gain, wait, scales=(1.0, 1.0)):
            toks = []
            for i, c0 in enumerate((0, 2)):
                b, = yield from grab(1)
                for c in (c0, c0 + 1):
                    for t in range(2):
                        k = tr(pb[b][:, (c - c0) * S + t * P:(c - c0) * S + (t + 1) * P],
                               src[:, t, c * P:(c + 1) * P], [T[key], bank_free[b]], inc=(c == c0 + 1 and t == 1))
                yield
                a = act(dst[:, c0:c0 + 2, :].rearrange("p c t -> p (c t)"), pb[b][:, :], ACT.Copy, [k, wait],
                        scale=scales[i] if gain is None else gain)
                give(b, a)
                toks.append(a)
            T[key + "_read"] = k
            T[key + "T"] = toks

        def turn_four(src, t, tok, c_at, T, key, gain=None):
            b, = yield from grab(1)
            for c in range(4):
                k = tr(pb[b][:, c * P:(c + 1) * P], src[:, c * P:(c + 1) * P], [tok, bank_free[b]], inc=(c == 3))
            yield
            o = pb[b][:, :].rearrange("p (c t) -> p c t", c=4)
            hh = HTh[:, c_at:c_at + 4, t * P:(t + 1) * P]
            hl = HTl[:, c_at:c_at + 4, t * P:(t + 1) * P]
            th = act(hh, o, ACT.Copy, [k, ht_free, t_hcol], scale=1.0 if gain is None else gain)
            if gain is None:
                tl = tt(hl, o, hh.bitcast(F32), ALU.subtract, [k, th, ht_free])
            else:
                tl = stt(hl, o, gain, hh.bitcast(F32), ALU.mult, ALU.subtract, [k, th, ht_free])
            give(b, tl)
            T[(key, t)] = [th, tl]

        def mixer1(layer, norm, following):
            ready = norm.ready
            fr = state["free1"]
            t_bc = state["t_bc1"]
            gq, gk = (hcol[:, 2 * layer + i:2 * layer + i + 1] for i in range(2))
            sq = part("sq", form="p (t n) -> p t n", t=2)
            sk = sbuf_h[:, 0, :, 0:128]
            sv = sbuf_h[:, 0, :, 128:256]
            kd = sbuf_h[:, 1, :, :].rearrange("p t (g u e) -> p t g u e", g=2, u=2)
            tmp = sbuf_s[:, :, :, :].rearrange("p a b c -> p (a b c)").rearrange("p (t n) -> p t n", t=2)
            sqT = part("sqT", form="p (c t) -> p c t", c=4)
            kT = part("kT", form="p (g t) -> p g t", g=2)
            qk = part("qk", form="p (t n) -> p t n", t=2)
            qkT = part("qkT", form="p (c t) -> p c t", c=4)
            vx = part("vx", form="p (t h e) -> p t h e", t=2, h=4)
            E = part("E", form="p (h n) -> p h n", h=4)
            pr0 = part("pr")[:, 0:1024].rearrange("p (h j) -> p h j", h=8)
            pr1 = part("pr")[:, 1024:3072].rearrange("p (h j) -> p h j", h=8)
            pt0 = part("prT")[:, 0:1024].rearrange("p (h j) -> p h j", h=8)
            pt1 = part("prT")[:, 1024:3072].rearrange("p (h s j) -> p h s j", h=8, s=2)
            mo = part("mo", form="p (t n) -> p t n", t=2)
            gab = part("gab", form="p (w t n) -> p w t n", w=2, t=2)
            arow = part("rows")[0:4, 0:256]
            mrow = part("rows")[0:4, 256:512]
            gz = col(16).rearrange("p (t n) -> p t n", t=2)
            T = {}
            pair = {"n": 0}

            def group(ncols):
                b0 = 2 * (pair["n"] % 2)
                pair["n"] += 1
                while b0 in held:
                    advance()
                banks = [[(b0 + t, 0, ncols)] for t in range(2)]
                done = product(XTh, XTl, list(range(KD)), ready, ncols, 2, banks)
                state["xt_free"] = [done[(1, 0)]]
                return b0, done

            def g_small():
                b0, done = group(264)
                T["gz"], T["skv"] = [], []
                r, r_tok = norm.r, norm.r_tok
                for t in range(2):
                    b = pb[b0 + t]
                    v = stt(gz[:, t, :], b[:, 0:8], r[:, t:t + 1], bcp1("gb"), ALU.mult, ALU.add,
                            [done[(t, 0)], r_tok, t_bc])
                    a = act(sbuf_h[:, 0, t, :], b[:, 8:264], ACT.Copy, [v, sh["h"]], scale=r[:, t:t + 1])
                    bank_free[b0 + t] = [a]
                    T["gz"].append(v)
                    T["skv"].append(a)

            def g_copy(dst, key, form=None):
                b0, done = group(512)
                toks = []
                for t in range(2):
                    src = pb[b0 + t][:, :]
                    if form is not None:
                        src = src.rearrange(form, h=4)
                    a = act(dst(t), src, ACT.Copy, [done[(t, 0)], norm.r_tok, fr], scale=norm.r[:, t:t + 1])
                    bank_free[b0 + t] = [a]
                    toks.append(a)
                T[key] = toks

            def g_query():
                b0, done = group(512)

                def chain():
                    yield from head_norm(b0, done, norm, sq, tmp, 0.125, [sh["s"], fr], T, "sq")
                    yield
                    yield from turn_two(sq, sqT, "sq", T, gq, [fr, t_hcol])

                chains.append(chain())

            def gates():
                f = gz[:, :, 4:8]
                e1, mx, nlf = (col(8).rearrange("p (t n) -> p t n", t=2) for _ in range(3))
                a = act(e1, f, ACT.Abs, [T["gz"]])
                a = act(e1, e1, ACT.Exp, [a], scale=-1.0)
                m = ts(mx, f, -1.0, 0.0, ALU.mult, ALU.max, [T["gz"]])
                yield
                v = ts(e1, e1, 1.0, None, ALU.add, after=[a])
                a = act(e1, e1, ACT.Ln, [v])
                yield
                nl = tt(nlf, e1, mx, ALU.add, [a, m])
                yield from pause(2)
                b, = yield from grab(1)
                o = pb[b][0:4, 0:256]
                w = [nl, T["gz"], t_tri, t_eye, bank_free[b]]
                for s in range(2):
                    mm(o, gz[:, s, 0:4], eye[:, s, :], s == 0, False, w)
                for s in range(2):
                    k = mm(o, nlf[:, s, :], tri[:, s, :], False, s == 1, inc=(s == 1))
                yield
                v = cp(arow, o, [k, fr])
                give(b, v)
                mt = VE.put(lambda e: e.tensor_tensor_scan(mrow, arow, arow, 0.0, ALU.max, ALU.max), [v])
                yield
                b, = yield from grab(1)
                for t in range(2):
                    for s in range(2):
                        mm(pb[b][:, 4 * t:4 * t + 4], tri[:, s, t * P:(t + 1) * P], nlf[:, s, :], s == 0, s == 1,
                           [v, mt, bank_free[b], nl])
                for i, row in enumerate((arow, mrow)):
                    for t in range(2):
                        k = tr(pb[b][:, 8 + 8 * i + 4 * t:12 + 8 * i + 4 * t], row[:, t * P:(t + 1) * P],
                               inc=(i == 1 and t == 1))
                yield
                tk = col(24)
                v = cp(tk, pb[b][:, 0:24], [k])
                give(b, v)
                em = col(8)
                w = tt(em, tk[:, 0:8], tk[:, 16:24], ALU.subtract, [v])
                for h0 in (0, 2):
                    b, = yield from grab(1)
                    for h in (h0, h0 + 1):
                        k = mm(pb[b][:, (h - h0) * S:(h - h0 + 1) * S], sel[0:4, h, :], mrow, True, True,
                               [mt, t_sel, bank_free[b]], inc=(h == h0 + 1))
                    yield
                    for h in (h0, h0 + 1):
                        m = pb[b][:, (h - h0) * S:(h - h0 + 1) * S]
                        stt(E[:, h, 0:256], m, tk[:, 8 + h:9 + h], cmask, ALU.subtract, ALU.max, [k, v, t_cm, fr])
                        x = stt(E[:, h, 256:384], m[:, P:2 * P], tk[:, 12 + h:13 + h], cmask[:, 0:P], ALU.subtract,
                                ALU.max)
                    give(b, x)
                yield
                T["em_ap"] = em
                T["em"] = act(em, em, ACT.Exp, [w])
                T["E"] = act(E, E, ACT.Exp, [x], scale=-1.0)

            def keys():
                sqr = sbuf_h[:, 1, :, 0:128]
                a = act(sqr, sk, ACT.Square, [T["skv"], sh["h"]])
                yield
                ssk = col(4)
                v = red(ssk.rearrange("p (t g) -> p t g", t=2), sqr.rearrange("p t (g e) -> p t g e", e=64), ALU.add, [a])
                rk, p = rstd(ssk, 4, 64, [v])
                yield
                kt = []
                for t in range(2):
                    k3 = headed(sk[:, t, :], 2)
                    for u in range(2):
                        w = tt(kd[:, t, :, u, :], k3, rk[:, 2 * t:2 * t + 2].unsqueeze(2).to_broadcast([P, 2, 64]),
                               ALU.mult, [p, sh["h"]])
                    kt.append(w)
                yield
                b, = yield from grab(1)
                for g in range(2):
                    for t in range(2):
                        k = tr(pb[b][:, g * S + t * P:g * S + (t + 1) * P],
                               kd[:, t, g, :, :].rearrange("p u e -> p (u e)"), [kt, bank_free[b]],
                               inc=(g == 1 and t == 1))
                yield
                v = act(kT.rearrange("p g t -> p (g t)"), pb[b][:, :], ACT.Copy, [k, fr, t_hcol], scale=gk)
                give(b, v)
                T["kd"], T["kT"] = kt, v

            def window(t):
                nk, j0 = (P, P) if t == 0 else (2 * P, 0)
                pr = pr0 if t == 0 else pr1
                per = 512 // nk
                yield from have(T, "kT", "sqT")
                yield from have(state, "t_bias")
                yield
                lg = []
                for i0 in range(0, 4, per):
                    bs = yield from grab(2)
                    ks = []
                    for par, b in enumerate(bs):
                        rows = slice(64 * par, 64 * par + 64)
                        for i in range(i0, i0 + per):
                            g = (2 * i + par) // 4
                            k = mm(pb[b][:, (i - i0) * nk:(i - i0 + 1) * nk], sqT[rows, i, t * P:(t + 1) * P],
                                   kT[rows, g, 0:nk], True, True, [T["kT"], T["sqT"], bank_free[b]],
                                   inc=(i == i0 + per - 1))
                        ks.append(k)
                    yield
                    for par, (b, k) in enumerate(zip(bs, ks)):
                        h0 = 4 * par + i0
                        v = tt(pr[:, h0:h0 + per, :], pb[b][:, :].rearrange("p (h j) -> p h j", h=per),
                               bias[:, h0:h0 + per, j0:256], ALU.add, [k, state["t_bias"], state["pr_free"]])
                        give(b, v)
                        lg.append(v)
                yield
                m, nm, den, es, rec = (col(8) for _ in range(5))
                v = red(m, pr, ALU.max, [lg])
                v = tt(m, m, bcp1("sink"), ALU.max, [v, t_bc])
                n = ts(nm, m, -1.0, None, ALU.mult, after=[v])
                v = tt(es, bcp1("sink"), m, ALU.subtract, [v])
                yield
                es_t = act(es, es, ACT.Exp, [v])
                for h in range(8):
                    if h == 4:
                        yield
                    a = act(pr[:, h, :], pr[:, h, :], ACT.Exp, [n], bias=nm[:, h:h + 1], acc=den[:, h:h + 1])
                T[("pr", t)] = a
                yield from pause(2)
                v = tt(den, den, es, ALU.add, [a, es_t])
                rt = recip(rec, den, [v])
                if t == 0:
                    sets = [[(h, 0) for h in range(h0, h0 + 4)] for h0 in (0, 4)]
                    flatT = pt0.rearrange("p h j -> p (h j)")
                else:
                    sets = [[(h, s) for h in (h0, h0 + 1) for s in range(2)] for h0 in (0, 2, 4, 6)]
                    flatT = pt1.rearrange("p h s j -> p (h s j)")
                pt = []
                for n, pieces in enumerate(sets):
                    b, = yield from grab(1)
                    for i, (h, s) in enumerate(pieces):
                        k = tr(pb[b][:, i * P:(i + 1) * P], pr[:, h, s * P:(s + 1) * P], [a, bank_free[b]], inc=(i == 3))
                    yield
                    o = flatT[:, n * 512:(n + 1) * 512]
                    v = act(o, pb[b][:, :], ACT.Copy, [k, fr]) if n % 2 else cp(o, pb[b][:, :], [k, fr])
                    give(b, v)
                    pt.append(v)
                T[("pr_read", t)] = k
                yield
                b, = yield from grab(1)
                for h in range(8):
                    i, par = h % 4, h // 4
                    g = (2 * i + par) // 4
                    o = pb[b][:, (2 * i + par) * 64:(2 * i + par + 1) * 64]
                    ns = 1 if t == 0 else 2
                    for s in range(ns):
                        l = pt0[:, h, :] if t == 0 else pt1[:, h, s, :]
                        k = mm(o, l, sv[:, s, g * 64:(g + 1) * 64], s == 0, s == ns - 1, [pt, T["skv"], bank_free[b]],
                               inc=(h == 7 and s == ns - 1))
                yield
                o4 = sq[:, t, :].rearrange("p (i a e) -> p i a e", i=4, a=2)
                src = pb[b][:, :].rearrange("p (i a e) -> p i a e", i=4, a=2)
                r4 = rec.rearrange("p (a i) -> p i a", a=2)
                for par in range(2):
                    v = tt(o4[:, :, par, :], src[:, :, par, :], r4[:, :, par].unsqueeze(2).to_broadcast([P, 4, 64]),
                           ALU.mult, [k, rt, T["sq_read"]])
                give(b, v)
                T[("hB", t)] = v
                yield
                yield from turn_four(sq[:, t, :], t, v, 4, T, "hBT")

            def scores():
                yield from have(T, "qk")
                yield
                yield from turn_two(qk, qkT, "qk", T, None, [fr], (1.0, 0.125))
                yield from have(T, "E")
                yield
                wt = []
                for h0 in (0, 2):
                    bs = yield from grab(2)
                    ks = []
                    for b, h in zip(bs, (h0, h0 + 1)):
                        rows = slice(64 * (h % 2), 64 * (h % 2) + 64)
                        q, kk = qkT[rows, h // 2, :], qkT[rows, 2 + h // 2, :]
                        mm(pb[b][:, 0:256], kk[:, 0:P], q, True, True, [T["qkT"], bank_free[b]])
                        ks.append(mm(pb[b][:, 256:384], kk[:, P:2 * P], q[:, P:2 * P], True, True, inc=True))
                    yield
                    for b, h, k in zip(bs, (h0, h0 + 1), ks):
                        v = tt(E[:, h, :], E[:, h, :], pb[b][:, 0:384], ALU.mult, [k, T["E"]])
                        give(b, v)
                        wt.append(v)
                T["Wt"] = wt

            def recall(t):
                yield from have(T, "Wt", "mv", "ones", "sq", "em")
                yield
                rec, dn, ss = col(4), col(4), col(4)
                bs = yield from grab(2)
                ks = []
                for b, h0 in zip(bs, (0, 2)):
                    for h in (h0, h0 + 1):
                        o = pb[b][:, (h - h0) * 129:(h - h0) * 129 + 129]
                        w = [T["Wt"], T["mv"], T["ones"], bank_free[b]]
                        k = mm(o, E[:, h, t * P:(t + 1) * P], vx[:, 0, h, :], True, t == 0, w,
                               inc=(t == 0 and h == h0 + 1))
                        if t == 1:
                            k = mm(o, E[:, h, 256:384], vx[:, 1, h, :], False, True, inc=(h == h0 + 1))
                    ks.append(k)
                yield
                num = [pb[b][:, 0:258].rearrange("p (h e) -> p h e", h=2) for b in bs]
                v = [cp(dn[:, h0:h0 + 2].unsqueeze(2), n[:, :, 128:129], [k]) for h0, n, k in zip((0, 2), num, ks)]
                v = stt(dn, dn, -1.0, dn, ALU.mult, ALU.max, [v])
                v = tt(dn, dn, T["em_ap"][:, 4 * t:4 * t + 4], ALU.max, [v, T["em"]])
                v = recip(rec, dn, [v])
                hs = []
                for b, h0, n in zip(bs, (0, 2), num):
                    w = tt(headed(qk[:, t, h0 * P:(h0 + 2) * P], 2), n[:, :, 0:128],
                           rec[:, h0:h0 + 2].unsqueeze(2).to_broadcast([P, 2, 128]), ALU.mult, [v, T["qk_read"]])
                    give(b, w)
                    hs.append(w)
                yield
                a = act(tmp[:, t, :], qk[:, t, :], ACT.Square, [hs, T["sq"]])
                yield
                v = red(ss, headed(tmp[:, t, :], 4), ALU.add, [a])
                rr, p = rstd(ss, 4, 128, [v])
                yield from have(T, "sig_mo")
                yield
                h3 = headed(qk[:, t, :], 4)
                v = tt(h3, h3, rr.unsqueeze(2).to_broadcast([P, 4, 128]), ALU.mult, [p])
                v = tt(qk[:, t, :], qk[:, t, :], bcp1("oln"), ALU.mult, [v, t_bc])
                v = tt(qk[:, t, :], qk[:, t, :], mo[:, t, :], ALU.mult, [v, T["sig_mo"]])
                T[("hA", t)] = v
                yield from pause(2)
                yield from turn_four(qk[:, t, :], t, v, 0, T, "hAT")

            def sigmoids():
                yield from have(T, "mo", ("pr", 0), ("pr", 1))
                yield
                T["sig_mo"] = act(mo, mo, ACT.Sigmoid, [T["mo"]])
                for w in range(2):
                    yield from have(T, f"g{w}0", f"g{w}1")
                    yield
                    T[("sig", w)] = act(gab[:, w, :, :], gab[:, w, :, :], ACT.Sigmoid, [T[f"g{w}0"], T[f"g{w}1"]])

            T["ones"] = PO.put(lambda e: e.memset(vx[:, :, :, 128:129], 1.0), [fr])
            g_copy(lambda t: qk[:, t, :], "qk")
            chains.append(scores())
            g_small()
            chains.extend([gates(), keys(), recall(0), recall(1)])
            if layer == 0:
                chains.append(bias_table())
            g_query()
            chains.extend([window(0), window(1), sigmoids()])
            g_copy(lambda t: vx[:, t, :, 0:128], "mv", form="p (h e) -> p h e")
            g_copy(lambda t: mo[:, t, :], "mo")
            for w in range(2):
                for n in range(2):
                    g_copy(lambda t: gab[:, w, t, n * 512:(n + 1) * 512], f"g{w}{n}")

            dA = product(HTh, HTl, [0, 1, 2, 3], lambda c, t: need(T, ("hAT", t)), 1024, 1, WIDE)
            drain()
            state["pr_free"] = [T[("pr_read", 1)]]
            for n in range(2):
                for t in range(2):
                    b = OB[t][n]
                    gs = gab[:, 0, t, n * 512:(n + 1) * 512]
                    v = tt(gs, gs, pb[b][:, :], ALU.mult, [dA[(t, n)], T[("sig", 0)]])
                    bank_free[b] = [v]
                    T[("a", t, n)] = v
            toks = {}

            def half(n, done):
                for t in range(2):
                    b = 4 + OB[t][n]
                    gs = gab[:, 1, t, n * 512:(n + 1) * 512]
                    v = tt(gs, gs, pb[b][:, :], ALU.mult, [done[t], T[("sig", 1)]])
                    bank_free[b] = [v]
                    T[("m", t, n)] = tt(gs, gs, gab[:, 0, t, n * 512:(n + 1) * 512], ALU.add, [v, T[("a", t, n)]])

            def mixed(lo, hi):
                for c in range(lo, hi):
                    turn_chunk(toks, c, lambda t: gab[:, 1, t, c * P:(c + 1) * P], lambda t: T[("m", t, c // 4)],
                               (4, 6, 0, 2, 5, 7, 4, 6)[c])()

            for n in range(2):
                done = product(HTh, HTl, [4, 5, 6, 7], lambda c, t: T[("hBT", t)], 512, 2,
                               [[(4 + OB[t][n], 0, 512)] for t in range(2)],
                               hook=(1, 1, lambda: mixed(0, 4)) if n == 1 else None)
                half(n, [done[(t, 0)] for t in range(2)])
            used = done[(1, 0)]
            for i in range(HT_SLOTS):
                ht_free[i] = [used]
            state["later"] = lambda: mixed(4, 8)
            state["xt_free"] = [into_x(XTh, XTl, list(range(KD)), lambda c, t: toks[c], 1.0, following)]
            sh["s"] = [[T[("hA", 0)], T[("hA", 1)]]] * 2
            sh["h"] = [[T[("hB", 0)], T[("hB", 1)]]] * 2
            state["free1"] = [x_tok[(1, 1)], toks[KD - 1], T[("hA", 0)], T[("hA", 1)]]

        def gated_input(layer, norm, following):
            tmp = part("gab", form="p (w t n) -> p w t n", w=2, t=2)
            dp = product(PTh, PTl, [0, 1], lambda c, t: state["pT"], 1024, 1, WIDE)

            def first_columns():
                for low in following.chunks(0, 4):
                    low()

            for n in range(2):
                bs = [4 + 2 * n + t for t in range(2)]
                dg = product(HTh, HTl, NormInHT.PLACE, norm.ready, 512, 2, [[(b, 0, 512)] for b in bs],
                             hook=(2, 0, first_columns) if n == 1 else None)
                for t in range(2):
                    o = tmp[:, 0, t, n * 512:(n + 1) * 512]
                    a = act(o, pb[bs[t]][:, :], ACT.Sigmoid, [dg[(t, 0)], norm.r_tok, state["free1"]],
                            scale=norm.r[:, t:t + 1])
                    bank_free[bs[t]] = [a]
                    v = tt(o, o, pb[OB[t][n]][:, :], ALU.mult, [a, dp[(t, n)]])
                    bank_free[OB[t][n]] = [v]
                    xs = X[:, t, n * 512:(n + 1) * 512]
                    x_tok[(t, n)] = [tt(xs, xs, o, ALU.add, [v, state["x_read"]])]
            for i in range(HT_SLOTS):
                ht_free[i] = [dg[(1, 0)]]
            state["later"] = following.rest
            state["free1"] = [x_tok[(1, 1)], dp[(1, 1)]]

        def load_ple(layer):
            return load(PO, part("gab")[:, 2048:2560].rearrange("p (k t) -> p k t", k=2), d["pT"][layer],
                        state["free1"])

        def split_ple(t_p):
            pin = part("gab")[:, 2048:2560].rearrange("p (k t) -> p k t", k=2)
            th = act(PTh[:, :, :], pin, ACT.Copy, [t_p, state["free1"]])
            tl = tt(PTl[:, :, :], pin, PTh[:, :, :].bitcast(F32), ALU.subtract, [th])
            state["pT"] = [th, tl]

        norm = Norm(0, TO_FFN)
        for low in norm.chunks(0, 4):
            low()
        state["later"] = norm.rest
        for layer in range(2):
            new_layer()
            small_inputs1(layer)
            after = Norm(4 * layer + 1, TO_MIX)
            ffn(norm, after)
            norm, after = after, Norm(4 * layer + 2, TO_FFN)
            mixer1(layer, norm, after)
            norm, after = after, NormInHT(4 * layer + 3, TO_MIX)
            t_pin = load_ple(layer)
            ffn(norm, after, lambda: split_ple(t_pin))
            norm, after = after, Norm(4 * layer + 4, AFTER_GATE)
            gated_input(layer, norm, after)
            norm = after
        first.close()

        c2, n2 = spans([("Pg", 2048), ("slope", 2048), ("bc", 1280), ("wg", 256), ("cw", 64), ("z", 512), ("zp", 572),
                        ("acc", 512), ("y", 2048), ("q", 1024), ("k", 1024), ("v", 1024), ("qT", 1024), ("kT", 1024),
                        ("up", 512), ("dT", 1024), ("pr", 4096), ("aT", 2048), ("yc", 512), ("tap", 1024)])
        scr2 = sb("scr2", [P, n2])
        fr1 = state["free1"]

        def part2(name, **kw):
            a = scr2[:, c2[name][0]:c2[name][1]]
            return a.rearrange(kw["form"], **{k: v for k, v in kw.items() if k != "form"}) if kw else a

        def bcp2(name):
            return part2("bc")[:, bc2[name][0]:bc2[name][1]]

        Pg = part2("Pg", form="p (g s t) -> p g s t", g=4, s=2)
        slope = part2("slope", form="p (h t k) -> p h t k", h=4, t=2)
        zp = part2("zp", form="p (c n) -> p c n", c=2)
        cw = part2("cw")
        wg = part2("wg", form="p (g n) -> p g n", g=4)
        state["free2"] = fr1

        def small_inputs2(layer):
            fr = state["free2"]
            state["t_bc2"] = load(PO, part2("bc"), d["bc2"][layer:layer + 1, :].to_broadcast([P, 1280]), fr)
            state["t_cw"] = load(PO, cw, d["cw"][layer], fr)
            state["t_wg"] = load(PO, wg[0:64, :, :], d["wg"][layer], fr)
            if layer == 0:
                state["t_slope"] = load(PO, slope, d["slope"], fr)
                state["t_pg"] = load(PO, Pg, d["Pg"], fr)
                state["z_pad"] = [PO.put(lambda e: e.memset(zp[:, :, 0:15], 0.0), [fr]),
                                  PO.put(lambda e: e.memset(zp[:, :, 271:286], 0.0), [fr])]
                state["post_gain"], state["post_tok"] = bcp2("post"), state["t_bc2"]
                state["pcol"] = tt(pcol[:, :], gcol[:, 14 * KD - KD * 3:14 * KD - KD * 2], postc[:, :], ALU.mult,
                                   [t_gcol, t_pcol])

        def mixer2(layer, norm, following):
            fr = state["free2"]
            lam0 = 0.8 - 0.6 * math.exp(-0.3 * layer)
            t_bc, t_cw, t_wg = state["t_bc2"], state["t_cw"], state["t_wg"]
            h0 = 4 + 9 * layer
            gq, gk, gs, gp0, gp1, lg0, lg1, lb0, lb1 = (hcol[:, h0 + i:h0 + i + 1] for i in range(9))
            z = part2("z", form="p (t n) -> p t n", t=2)
            acc = part2("acc", form="p (c t) -> p c t", c=2)
            yc = part2("yc", form="p (c t) -> p c t", c=2)
            y = part2("y", form="p (t n) -> p t n", t=2)
            q, k_, v_ = (part2(n, form="p (t n) -> p t n", t=2) for n in ("q", "k", "v"))
            qT, kT = (part2(n, form="p (c t) -> p c t", c=4) for n in ("qT", "kT"))
            up = part2("up", form="p (t n) -> p t n", t=2)
            dT = part2("dT", form="p (g t) -> p g t", g=4)
            pr = part2("pr", form="p (t m j) -> p t m j", t=2, m=8)
            aT = part2("aT", form="p (t n) -> p t n", t=2)
            tmp = sbuf_s[:, :, :, :].rearrange("p a b c -> p (a b c)").rearrange("p (t n) -> p t n", t=2)
            tmp2 = sbuf_h[:, :, :, :].rearrange("p a b c -> p (a b c)").rearrange("p (t n) -> p t n", t=2)
            taps = part2("tap", form="p (i t) -> p i t", i=4)
            T = {}
            pair = {"n": 0}

            def group(ncols, kper=2):
                b0 = 2 * (pair["n"] % 2)
                pair["n"] += 1
                while b0 in held:
                    advance()
                banks = [[(b0 + t, 0, ncols)] for t in range(2)]
                done = product(XTh, XTl, list(range(KD)), norm.ready, ncols, kper, banks)
                state["xt_free"] = [done[(1, 0)]]
                return b0, done

            def g_copy(dst_, key, ncols=512, kper=2):
                b0, done = group(ncols, kper)
                toks = []
                for t in range(2):
                    a = act(dst_[:, t, :], pb[b0 + t][:, 0:ncols], ACT.Copy, [done[(t, 0)], norm.r_tok, fr],
                            scale=norm.r[:, t:t + 1])
                    bank_free[b0 + t] = [a]
                    toks.append(a)
                T[key] = toks

            def g_head(dst_, key, buf, extra, before, dstT, gain):
                b0, done = group(512)
                wait = need(T, before) if before else sh["h"]

                def chain():
                    yield from head_norm(b0, done, norm, dst_, buf, extra, [wait, fr], T, key)
                    yield from pause(2)
                    yield from turn_two(dst_, dstT, key, T, gain, [fr, t_hcol])

                chains.append(chain())

            def lam():
                lr = bcp2("lam").rearrange("p (a b e) -> p a b e", a=2, b=2)
                pl = col(128).rearrange("p (a e) -> p a e", a=2)
                v = tt(pl, lr[:, :, 0, :], lr[:, :, 1, :], ALU.mult, [t_bc])
                s2 = col(2)
                v = red(s2, pl, ALU.add, [v])
                yield
                a = act(s2, s2, ACT.Exp, [v])
                yield
                nl = col(1)
                v = tt(nl, s2[:, 1:2], s2[:, 0:1], ALU.subtract, [a])
                T["nlam_ap"] = nl
                T["nlam"] = ts(nl, nl, -lam0, None, ALU.add, after=[v])

            def g_conv():
                b0, done = group(512)
                zs = []
                for t in range(2):
                    b = pb[b0 + t]
                    a = act(tmp[:, t, 0:256], b[:, 256:512], ACT.Sigmoid, [done[(t, 0)], norm.r_tok, sh["s"]],
                            scale=norm.r[:, t:t + 1])
                    v = stt(z[:, t, :], b[:, 0:256], norm.r[:, t:t + 1], tmp[:, t, 0:256], ALU.mult, ALU.mult, [a, fr])
                    bank_free[b0 + t] = [v]
                    zs.append(v)
                T["z"] = zs

            def conv():
                yield
                b, = yield from grab(1)
                for c in range(2):
                    for t in range(2):
                        k = tr(pb[b][:, c * S + t * P:c * S + (t + 1) * P], z[:, t, c * P:(c + 1) * P],
                               [T["z"], bank_free[b]], inc=(c == 1 and t == 1))
                yield
                a = act(zp[:, :, 15:271], pb[b][:, :].rearrange("p (c t) -> p c t", c=2), ACT.Copy, [k, fr])
                give(b, a)
                T["z_read"] = k
                yield
                w = [a, state["z_pad"], t_cw, fr]
                for j in range(31):
                    s0, s1 = zp[:, 0, j:j + S], zp[:, 1, j:j + S]
                    w0, w1 = cw[:, j:j + 1], cw[:, 31 + j:32 + j]
                    if j == 0:
                        v = ts(acc[:, 0, :], s0, w0, cw[:, 62:63], ALU.mult, ALU.add, w)
                        p = act(acc[:, 1, :], s1, ACT.Identity, w, scale=w1, bias=cw[:, 63:64])
                    else:
                        v = stt(acc[:, 0, :], s0, w0, acc[:, 0, :], ALU.mult, ALU.add, [v])
                        T[("tap", j)] = m = act(taps[:, j % 4, :], s1, ACT.Copy, [T.get(("added", j - 4)), w], scale=w1)
                        add = [p, m]
                        T[("added", j)] = p = PO.put(
                            lambda e, j=j: e.tensor_tensor(acc[:, 1, :], acc[:, 1, :], taps[:, j % 4, :], ALU.add), add)
                    if j % 2 == 0:
                        yield
                b, = yield from grab(1)
                for t in range(2):
                    for c in range(2):
                        k = tr(pb[b][:, t * S + c * P:t * S + (c + 1) * P], acc[:, c, t * P:(t + 1) * P],
                               [v, p, bank_free[b]], inc=(c == 1 and t == 1))
                yield
                mu, nmu, ss, sh_ = (col(2) for _ in range(4))
                for t in range(2):
                    a = act(z[:, t, :], pb[b][:, t * S:(t + 1) * S], ACT.Copy, [k, T["z_read"]], acc=mu[:, t:t + 1])
                give(b, a)
                yield
                v = ts(nmu, mu, -1.0 / 256, None, ALU.mult, after=[a])
                for t in range(2):
                    a = act(tmp[:, t, 0:256], z[:, t, :], ACT.Square, [v, a], bias=nmu[:, t:t + 1], acc=ss[:, t:t + 1])
                yield
                rr, p = rstd(ss, 2, 256, [a])
                yield
                v = tt(sh_, nmu, rr, ALU.mult, [p])
                for t in range(2):
                    a = act(z[:, t, :], z[:, t, :], ACT.Identity, [v], scale=rr[:, t:t + 1], bias=sh_[:, t:t + 1])
                T["zn"] = a
                yield
                b, = yield from grab(1)
                for c in range(2):
                    for t in range(2):
                        k = tr(pb[b][:, c * S + t * P:c * S + (t + 1) * P], z[:, t, c * P:(c + 1) * P],
                               [a, bank_free[b]], inc=(c == 1 and t == 1))
                yield
                for c, (g, bb) in enumerate(((lg0, lb0), (lg1, lb1))):
                    a = act(yc[:, c, :], pb[b][:, c * S:(c + 1) * S], ACT.Silu, [k, t_hcol, fr], scale=g, bias=bb)
                give(b, a)
                th = act(HTh[:, 0:2, :], yc, ACT.Copy, [a, ht_free])
                yield
                tl = tt(HTl[:, 0:2, :], yc, HTh[:, 0:2, :].bitcast(F32), ALU.subtract, [th, ht_free])
                T["conv"] = [th, tl]

            def pool():
                ds = []
                for g0 in (0, 2):
                    b, = yield from grab(1)
                    for g in (g0, g0 + 1):
                        for s in range(2):
                            k = mm(pb[b][0:64, (g - g0) * S:(g - g0 + 1) * S], up[:, s, g * 64:(g + 1) * 64],
                                   Pg[:, g, s, :], s == 0, s == 1, [T["up"], state["t_pg"], bank_free[b]],
                                   inc=(g == g0 + 1 and s == 1))
                    yield
                    a = act(dT[0:64, g0:g0 + 2, :].rearrange("p g t -> p (g t)"), pb[b][0:64, :], ACT.Copy, [k, fr])
                    give(b, a)
                    ds.append(a)
                yield
                b, = yield from grab(1)
                for t in range(2):
                    for g in range(4):
                        k = mm(pb[b][:, t * S + g * 64:t * S + (g + 1) * 64], dT[0:64, g, t * P:(t + 1) * P],
                               wg[0:64, g, :], True, True, [ds, t_wg, bank_free[b]], inc=(t == 1 and g == 3))
                yield
                a = act(y[:, :, 256:512], pb[b][:, :].rearrange("p (t n) -> p t n", t=2), ACT.Copy, [k, fr])
                give(b, a)
                yield
                b, = yield from grab(1)
                for c in range(2):
                    for t in range(2):
                        k = tr(pb[b][:, c * S + t * P:c * S + (t + 1) * P], y[:, t, (2 + c) * P:(3 + c) * P],
                               [a, bank_free[b]], inc=(c == 1 and t == 1))
                yield
                th = [act(HTh[:, 2 + c, :], pb[b][:, c * S:(c + 1) * S], ACT.Copy, [k, ht_free, t_hcol],
                          scale=(gp0, gp1)[c]) for c in range(2)]
                for c in range(2):
                    tl = stt(HTl[:, 2 + c, :], pb[b][:, c * S:(c + 1) * S], (gp0, gp1)[c],
                             HTh[:, 2 + c, :].bitcast(F32), ALU.mult, ALU.subtract, [th])
                give(b, tl)
                T["pool"] = [th, tl]

            def maps(t):
                m, n, den, rec, ss = (col(8) for _ in range(5))
                yield from have(T, "qT", "kT")
                yield from pause(1 + 3 * t)
                lg = []
                for h0 in (0, 2):
                    bs = yield from grab(2)
                    ks = []
                    for h in (h0, h0 + 1):
                        for c in range(2):
                            rows = slice(64 * c, 64 * c + 64)
                            ks.append(mm(pb[bs[c]][:, (h - h0) * S:(h - h0 + 1) * S], qT[rows, h, t * P:(t + 1) * P],
                                         kT[rows, h, :], True, True, [T["qT"], T["kT"], bank_free[bs[c]]],
                                         inc=(h == h0 + 1)))
                    yield
                    for c in range(2):
                        for h in (h0, h0 + 1):
                            i = 4 * c + h
                            src = pb[bs[c]][:, (h - h0) * S:(h - h0 + 1) * S]
                            v = VE.put(lambda e, i=i, h=h, src=src: e.tensor_tensor_reduce(
                                pr[:, t, i, :], src, slope[:, h, t, :], 1.0, NEG, ALU.add, ALU.max, m[:, i:i + 1]),
                                [ks[2 + c], state["t_slope"], fr])
                            lg.append(v)
                        give(bs[c], v)
                v = ts(n, m, -1.0, None, ALU.mult, after=[lg])
                yield
                for i in (0, 4, 1, 5, 2, 6, 3, 7):
                    if i == 2:
                        yield
                    a = act(pr[:, t, i, :], pr[:, t, i, :], ACT.Exp, [v], bias=n[:, i:i + 1], acc=den[:, i:i + 1])
                yield from pause(3)
                yield from have(T, "nlam", "v")
                v = recip(rec, den, [a])
                v = tt(rec[:, 4:8], rec[:, 4:8], den[:, 0:4], ALU.mult, [v])
                v = ts(rec[:, 4:8], rec[:, 4:8], T["nlam_ap"], None, ALU.mult, after=[v, T["nlam"]])
                at_ = []
                for h0 in (0, 2):
                    for h in (h0, h0 + 1):
                        x = stt(pr[:, t, h, :], pr[:, t, 4 + h, :], rec[:, 4 + h:5 + h], pr[:, t, h, :],
                                ALU.mult, ALU.add, [v])
                    yield
                    b, = yield from grab(1)
                    for i, (h, s) in enumerate([(h, s) for h in (h0, h0 + 1) for s in range(2)]):
                        k = tr(pb[b][:, i * P:(i + 1) * P], pr[:, t, h, s * P:(s + 1) * P], [x, bank_free[b]],
                               inc=(i == 3))
                    yield
                    a = act(aT[:, t, (h0 // 2) * 512:(h0 // 2 + 1) * 512], pb[b][:, :], ACT.Copy, [k, fr])
                    give(b, a)
                    at_.append(a)
                yield
                b, = yield from grab(1)
                for h in range(4):
                    for s in range(2):
                        k = mm(pb[b][:, h * P:(h + 1) * P], aT[:, t, (2 * h + s) * P:(2 * h + s + 1) * P],
                               v_[:, s, h * P:(h + 1) * P], s == 0, s == 1, [at_, T["v"], bank_free[b]],
                               inc=(h == 3 and s == 1))
                yield
                a = act(tmp2[:, t, :], pb[b][:, :], ACT.Square, [k, sh["h"], T["q"], T["k"]])
                yield
                x = red(ss[:, 0:4], headed(tmp2[:, t, :], 4), ALU.add, [a])
                x = tt(ss[:, 0:4], ss[:, 0:4], rec[:, 0:4], ALU.mult, [x])
                x = tt(ss[:, 0:4], ss[:, 0:4], rec[:, 0:4], ALU.mult, [x])
                rr, p = rstd(ss[:, 0:4], 4, 128, [x], 1.0 - lam0)
                yield
                x = tt(rr, rr, rec[:, 0:4], ALU.mult, [p])
                x = tt(headed(y[:, t, 512:1024], 4), headed(pb[b][:, :], 4),
                       rr.unsqueeze(2).to_broadcast([P, 4, 128]), ALU.mult, [x, a, fr])
                give(b, x)
                T[("y", t)] = x
                yield
                yield from turn_four(y[:, t, 512:1024], t, x, 4, T, "yT", gs)

            state["halves"] = True
            chains.append(lam())
            g_head(q, "q", tmp2, 0.125, None, qT, gq)
            g_head(k_, "k", tmp2, 1.0, "q", kT, gk)
            chains.extend([maps(0), maps(1)])
            g_conv()
            chains.append(conv())
            g_copy(v_, "v")
            g_copy(up, "up", 256, 4)
            chains.append(pool())

            def ready(c, t):
                return need(T, "conv" if c < 2 else "pool" if c < 4 else ("yT", t))

            state["halves"] = False
            used = into_x(HTh, HTl, OUT2, ready, 1.0, following)
            for i in range(HT_SLOTS):
                ht_free[i] = [used]
            last = [T[("y", 0)], T[("y", 1)], T["zn"]]
            sh["s"] = [last, last]
            sh["h"] = [last, last]
            state["free2"] = [x_tok[(1, 1)], used, last, T["pool"], T["conv"]]

        def post():
            ss = col(2)
            a = square_sum(ss)
            rr, p = rstd(ss, 2, D, [a])
            for t in range(2):
                v = stt(X[:, t, :], X[:, t, :], rr[:, t:t + 1], bcp2("post"), ALU.mult, ALU.mult, [p, state["t_bc2"]])
                x_tok[(t, 0)] = x_tok[(t, 1)] = [v]

        t_pcol = load(PO, postc[:, :], d["postc"])
        for layer in range(2):
            new_layer()
            if layer == 0:
                small_inputs2(0)
            after = Norm(8 + 3 * layer + 1, TO_MIX)
            if layer == 0:
                ffn(norm, after)
            else:
                ffn(norm, after, lambda: small_inputs2(1))
            norm, after = after, Norm(8 + 3 * layer + 2, TO_FFN)
            mixer2(layer, norm, after)
            norm = after
            after = NormTwice(0, TO_FFN, pcol[:, :], state["pcol"]) if layer == 0 else None
            ffn(norm, after)
            norm = after
            if layer == 0:
                state["free2"] = [state["free2"], x_tok[(1, 1)]]
        post()
        s_out = sem("s_out")
        for t in range(2):
            SP.put(lambda e, t=t: e.dma_start(out[t * P:(t + 1) * P, :], X[:, t, :]), [x_tok[(t, 0)]],
                   signal=(s_out, 16))
        assert at["use"] == n_units

        block = ctx.enter_context(nc.Block())

        @block.tensor
        def _(eng):
            PE.run(eng)

        @block.vector
        def _(eng):
            VE.run(eng)

        @block.scalar
        def _(eng):
            SE.run(eng)

        @block.gpsimd
        def _(eng):
            PO.run(eng)

        @block.sync
        def _(eng):
            SP.run(eng)
            eng.wait_ge(s_out, 32)


def bucket(dist):
    half = 16
    dd = np.maximum(dist, 0)
    large = half + (np.log(np.maximum(dd, 1) / half) / np.log(128 / half) * half).astype(np.int32)
    return np.where(dd < half, dd, np.minimum(large, 31)).astype(np.int32)


def constants():
    f = np.float32
    i = np.arange(S)
    ident = np.eye(P, dtype=f)
    tri = (i[:, None] <= i[None, :]).astype(f).reshape(2, P, S).transpose(1, 0, 2)
    eye = np.eye(S, dtype=f).reshape(2, P, S).transpose(1, 0, 2)
    cmask = np.zeros((P, S), f)
    cmask[:, :P] = np.where(np.arange(P)[:, None] <= np.arange(P)[None, :], 0.0, -NEG)
    sel = np.zeros((4, 4, P), f)
    for h in range(4):
        sel[h, h, :] = 1.0
    n = np.arange(384)
    dist = P - np.where(n < 256, n, n - 384)
    ok = (dist >= 0) & (dist < P)
    onehot = np.zeros((33, 384), f)
    onehot[bucket(dist), n] = 1.0
    onehot[:, ~ok] = 0.0
    onehot[32] = np.where(ok, 0.0, NEG)
    Pg = np.zeros((4, S, S), f)
    for g, w in enumerate((2, 4, 8, 16)):
        for t in range(S):
            lo, hi = max(t - w // 2, 0), min(t + w // 2, S)
            Pg[g, lo:hi, t] = f(1.0) / f(hi - lo)
            Pg[g, t, t] -= f(1.0)
    Pg = Pg.reshape(4, 2, P, S).transpose(2, 0, 1, 3)
    dd = np.abs(i[:, None] - i[None, :]).astype(f).reshape(2, P, S).transpose(1, 0, 2)
    slope = np.stack([-dd * f(2.0 ** (-8.0 * (h + 1) / 4)) for h in range(4)], 1)
    return {k: np.ascontiguousarray(v, dtype=f) for k, v in
            dict(ident=ident, tri=tri, eye=eye, cmask=cmask, sel=sel, onehot=onehot, Pg=Pg, slope=slope).items()}


def layout(a):
    units = []

    def rows(w, c0, c1, k0, n):
        return w[k0 * P:(k0 + n) * P, c0:c1].reshape(n, P, c1 - c0).transpose(1, 0, 2)

    def group(w, kper):
        for k0 in range(0, w.shape[0] // P, kper):
            units.append(rows(w, 0, w.shape[1], k0, kper).reshape(P, -1))

    def ffn(wg, wu, wo):
        for kind, g in ffn_order():
            if kind == "gu":
                for k0 in range(0, KD, 2):
                    u = np.stack([rows(wg, 256 * g, 256 * g + 256, k0, 2), rows(wu, 256 * g, 256 * g + 256, k0, 2)], 2)
                    units.append(u.reshape(P, -1))
            else:
                group(wo[256 * g:256 * g + 256], 1)

    for i in range(2):
        wi = a["ffn1_wi"][i]
        ffn(wi[:, :FF], wi[:, FF:], a["ffn1_wo"][i])
        w = a["w_in"][i]
        mq, mk, mv, mo, gi, sq, skv, ga, gb = np.split(w, [256, 512, 1024, 1536, 1544, 2056, 2312, 3336], axis=1)
        group(np.concatenate([mq, mk], 1), 2)
        group(np.concatenate([gi, skv], 1), 2)
        group(sq, 2)
        group(mv, 2)
        group(mo, 2)
        for x in (ga, gb):
            group(x[:, :512], 2)
            group(x[:, 512:], 2)
        group(a["w_a"][i], 1)
        group(a["w_b"][i][:, :512], 2)
        group(a["w_b"][i][:, 512:], 2)
        group(a["w_out"][i], 1)
        wi = a["ffn2_wi"][i]
        ffn(wi[:, :FF], wi[:, FF:], a["ffn2_wo"][i])
        group(a["w_ple"][i], 1)
        group(a["w_ple_gate"][i][:, :512], 2)
        group(a["w_ple_gate"][i][:, 512:], 2)
    for i in range(2):
        ffn(a["ffn1_w_gate_2"][i], a["ffn1_w_up_2"][i], a["ffn1_w_down_2"][i])
        conv, pool, q, k, v = np.split(a["w_in_2"][i], [512, 768, 1280, 1792], axis=1)
        group(q, 2)
        group(k, 2)
        group(conv, 2)
        group(v, 2)
        group(pool, 4)
        group(a["w_out_2"][i].reshape(KD, P, D)[OUT2].reshape(D, D), 1)
        ffn(a["ffn2_w_gate_2"][i], a["ffn2_w_up_2"][i], a["ffn2_w_down_2"][i])
    cols = [u.shape[1] for u in units]
    W = np.zeros((len(units), P, UC), np.float32)
    for n, u in enumerate(units):
        W[n, :, :cols[n]] = u
    return W, cols


def kernel(**inputs):
    import concourse.bacc as bacc
    from concourse.bass_utils import run_bass_kernel_spmd as run

    a = {k: np.asarray(v) for k, v in inputs.items()}
    heads = [0, 2, 4, 6, 1, 3, 5, 7]

    def columns(v):
        return v.reshape(KD, P).T

    W, cols = layout(a)
    gains = []
    for i in range(2):
        gains += [a[n][i] for n in ("ffn1_norm", "mix_norm", "ffn2_norm", "ple_norm")]
    for i in range(2):
        gains += [a[n][i] for n in ("ffn1_norm_2", "mix_norm_2", "ffn2_norm_2")]
    bc1 = np.stack([np.concatenate([a["ml_out_norm"][i].reshape(-1), a["sinks"][i][heads], a["b_igate"][i],
                                    a["b_fgate"][i]]) for i in range(2)])
    bc2 = np.stack([np.concatenate([a["post_norm_2"][i], a["lambda_q1_2"][i], a["lambda_k1_2"][i],
                                    a["lambda_q2_2"][i], a["lambda_k2_2"][i]]) for i in range(2)])
    hcol = []
    for i in range(2):
        hcol += [np.tile(a["q_norm"][i], 2), np.tile(a["k_norm"][i], 2)]
    for i in range(2):
        hcol += [np.tile(a["q_norm_2"][i], 2), np.tile(a["k_norm_2"][i], 2), a["attn_subln_2"][i]]
        hcol += list(a["pool_scale_2"][i].reshape(2, P)) + list(a["conv_ln_gain_2"][i].reshape(2, P))
        hcol += list(a["conv_ln_bias_2"][i].reshape(2, P))
    cw = np.stack([np.concatenate([a["conv_dw_2"][i].reshape(31, 2, P).transpose(2, 1, 0).reshape(P, 62),
                                   a["conv_dw_bias_2"][i].reshape(2, P).T], 1) for i in range(2)])
    arrays = dict(constants())
    arrays.update(
        W=W,
        x=a["x"][0].reshape(2, P, D).transpose(1, 0, 2),
        gcol=np.concatenate([columns(g) for g in gains], 1),
        bc1=bc1, bc2=bc2, cw=cw, hcol=np.stack(hcol, 1), postc=columns(a["post_norm_2"][0]),
        rb=np.repeat(a["rel_bias"][:, heads], P, axis=1).reshape(32, 8, P),
        pT=np.stack([a["p"][i, 0].T.reshape(2, P, S).transpose(1, 0, 2) for i in range(2)]),
        wg=a["pool_w_2"].transpose(0, 2, 1, 3),
    )
    arrays = {k: np.ascontiguousarray(v) for k, v in arrays.items()}
    nc = bacc.Bacc("TRN2", target_bir_lowering=False, num_devices=1)
    d = {k: nc.dram_tensor("in_" + k, v.shape, F32, kind="ExternalInput").ap() for k, v in arrays.items()}
    d["scratch"] = nc.dram_tensor("scratch", (8, P, 384), F32, kind="Internal").ap()
    d["cols"] = cols
    out = nc.dram_tensor("out_0", (S, D), F32, kind="ExternalOutput").ap()
    program(nc, d, out)
    r = run(nc, [{"in_" + k: v for k, v in arrays.items()}], core_ids=[0])
    return np.asarray(r.results[0]["out_0"]).reshape(1, S, D)
```
